# Optimizing a Trainium2 kernel written in Bass

```python
import jax, jax.numpy as jnp
from jax import lax
import numpy as np

D_MODEL = 1024
BATCH = 1
SEQ = 512
DEPTH = 1

W_A = 512
A_GROUPS = 8
A_CONV = 3
W_B = 1024
LRU_HEADS = 8
LRU_HEAD_DIM = W_B // LRU_HEADS
B_CONV = 4
LRU_C = 8.0
W_C = 512
POOL_WINDOWS = (2, 4, 8, 16)
POOL_GROUPS = len(POOL_WINDOWS)
POOL_GROUP_DIM = W_C // POOL_GROUPS
N_BRANCH = 3
SPLITS = [W_A, 2 * W_A, 3 * W_A, 3 * W_A + W_B, 3 * W_A + 2 * W_B,
          3 * W_A + 2 * W_B + W_C, 3 * W_A + 2 * W_B + W_C + D_MODEL,
          3 * W_A + 2 * W_B + W_C + 2 * D_MODEL]
IN_COLS = 3 * W_A + 2 * W_B + W_C + N_BRANCH * D_MODEL
N_GROUPS = 4
EXPERTS_PER_GROUP = 4
N_EXPERTS = N_GROUPS * EXPERTS_PER_GROUP
TOP_K = 2
D_EXPERT = 512
EPS = 1e-6

kernel_name = "hybrid_conv_lru_pool_hmoe"

def rmsnorm(x, g):
    xf = x.astype(jnp.float32)
    y = xf * lax.rsqrt(jnp.mean(xf * xf, axis=-1, keepdims=True) + EPS)
    return (y * g.astype(jnp.float32)).astype(x.dtype)

def causal_dwconv(x, w):
    k, c = w.shape
    return lax.conv_general_dilated(
        x, w[:, None, :].astype(x.dtype), window_strides=(1,), padding=[(k - 1, 0)],
        dimension_numbers=("NWC", "WIO", "NWC"), feature_group_count=c)

def rg_lru(x, w_a, b_a, w_x, b_x, lam):
    bsz, s, w = x.shape
    xh = x.reshape(bsz, s, LRU_HEADS, LRU_HEAD_DIM)
    r = jax.nn.sigmoid(jnp.einsum("bshi,hij->bshj", xh, w_a) + b_a).reshape(bsz, s, w)
    i = jax.nn.sigmoid(jnp.einsum("bshi,hij->bshj", xh, w_x) + b_x).reshape(bsz, s, w)
    log_a = -LRU_C * r.astype(jnp.float32) * jax.nn.softplus(-lam.astype(jnp.float32))
    a = jnp.exp(log_a)
    b = jnp.sqrt(-jnp.expm1(2.0 * log_a)) * (i * x).astype(jnp.float32)

    def combine(left, right):
        a_l, b_l = left
        a_r, b_r = right
        return a_r * a_l, a_r * b_l + b_r

    _, h = lax.associative_scan(combine, (a, b), axis=1)
    return h.astype(x.dtype)

def multiscale_pool(u):
    s = u.shape[1]
    cs = jnp.cumsum(u.astype(jnp.float32), axis=1)
    t = jnp.arange(1, s + 1, dtype=jnp.float32)
    outs = []
    for g, w in enumerate(POOL_WINDOWS):
        c = cs[..., g * POOL_GROUP_DIM:(g + 1) * POOL_GROUP_DIM]
        lag = jnp.pad(c, ((0, 0), (w, 0), (0, 0)))[:, :s]
        cnt = jnp.minimum(t, float(w))[None, :, None]
        outs.append((c - lag) / cnt)
    pooled = jnp.concatenate(outs, axis=-1)
    return (pooled - u.astype(jnp.float32)).astype(u.dtype)

def mixer_sublayer(h, w_in, conv_a_w, w_a_out, conv_b_w, conv_b_b, lru_wa, lru_ba,
                   lru_wx, lru_bx, lru_lambda, w_b_out, pool_w, pool_scale, w_c_out, w_o):
    bsz, s, _ = h.shape
    z = h @ w_in
    a_b, a_c, a_x, b_x, b_y, c_u, g_a, g_b, g_c = jnp.split(z, SPLITS, axis=-1)
    y_a = a_b * causal_dwconv(a_c * a_x, conv_a_w)
    xb = causal_dwconv(b_x, conv_b_w) + conv_b_b
    y_b = rg_lru(xb, lru_wa, lru_ba, lru_wx, lru_bx, lru_lambda) * jax.nn.gelu(b_y)
    pc = multiscale_pool(c_u).reshape(bsz, s, POOL_GROUPS, POOL_GROUP_DIM)
    y_c = jnp.einsum("bsgi,gij->bsgj", pc, pool_w).reshape(bsz, s, W_C) * pool_scale
    m = (jax.nn.sigmoid(g_a) * (y_a @ w_a_out)
         + jax.nn.sigmoid(g_b) * (y_b @ w_b_out)
         + jax.nn.sigmoid(g_c) * (y_c @ w_c_out))
    return m @ w_o

def hier_moe(h, w_grp, b_grp, w_exp, b_exp, w1, w3, w2):
    bsz, s, d = h.shape
    t = h.reshape(-1, d)
    n_tok = t.shape[0]
    grp_prob = jax.nn.softmax((t @ w_grp + b_grp).astype(jnp.float32), axis=-1)
    g_p, g_idx = lax.top_k(grp_prob, 1)
    exp_logits = (t @ w_exp + b_exp).astype(jnp.float32).reshape(n_tok, N_GROUPS, EXPERTS_PER_GROUP)
    sel = jnp.take_along_axis(exp_logits, g_idx[:, :, None], axis=1)[:, 0]
    e_val, e_idx = lax.top_k(sel, TOP_K)
    e_w = jax.nn.softmax(e_val, axis=-1) * g_p
    within = jnp.sum(jax.nn.one_hot(e_idx, EXPERTS_PER_GROUP, dtype=jnp.float32) * e_w[..., None], axis=1)
    gate = (jax.nn.one_hot(g_idx[:, 0], N_GROUPS, dtype=jnp.float32)[:, :, None]
            * within[:, None, :]).reshape(n_tok, N_EXPERTS).astype(h.dtype)
    out = jnp.zeros_like(t)
    for e in range(N_EXPERTS):
        hid = jax.nn.silu(t @ w1[e]) * (t @ w3[e])
        out = out + gate[:, e:e + 1] * (hid @ w2[e])
    return out.reshape(bsz, s, d)

def setup_inputs(seed: int = 0) -> dict:
    key = jax.random.key(seed)
    ks = jax.random.split(key, 32)

    def nrm(k, shape, scale):
        return jax.random.normal(k, shape, jnp.float32) * scale

    L, D = DEPTH, D_MODEL
    u = jax.random.uniform(ks[12], (L, W_B), jnp.float32, minval=0.9, maxval=0.999)
    sig = u ** (1.0 / LRU_C)
    lam = jnp.log(sig) - jnp.log1p(-sig)
    return {
        "x": nrm(ks[0], (BATCH, SEQ, D), 1.0),
        "norm1_g": 1.0 + nrm(ks[1], (L, D), 0.02),
        "w_in": nrm(ks[2], (L, D, IN_COLS), D ** -0.5),
        "conv_a_w": nrm(ks[3], (L, A_CONV, W_A), A_CONV ** -0.5),
        "w_a_out": nrm(ks[4], (L, W_A, D), W_A ** -0.5),
        "conv_b_w": nrm(ks[5], (L, B_CONV, W_B), B_CONV ** -0.5),
        "conv_b_b": nrm(ks[6], (L, W_B), 0.01),
        "lru_wa": nrm(ks[7], (L, LRU_HEADS, LRU_HEAD_DIM, LRU_HEAD_DIM), LRU_HEAD_DIM ** -0.5),
        "lru_ba": nrm(ks[8], (L, LRU_HEADS, LRU_HEAD_DIM), 0.01),
        "lru_wx": nrm(ks[9], (L, LRU_HEADS, LRU_HEAD_DIM, LRU_HEAD_DIM), LRU_HEAD_DIM ** -0.5),
        "lru_bx": nrm(ks[10], (L, LRU_HEADS, LRU_HEAD_DIM), 0.01),
        "lru_lambda": lam,
        "w_b_out": nrm(ks[11], (L, W_B, D), W_B ** -0.5),
        "pool_w": nrm(ks[13], (L, POOL_GROUPS, POOL_GROUP_DIM, POOL_GROUP_DIM), POOL_GROUP_DIM ** -0.5),
        "pool_scale": 1.0 + nrm(ks[14], (L, W_C), 0.02),
        "w_c_out": nrm(ks[15], (L, W_C, D), W_C ** -0.5),
        "w_o": nrm(ks[16], (L, D, D), D ** -0.5),
        "norm2_g": 1.0 + nrm(ks[17], (L, D), 0.02),
        "router_grp_w": nrm(ks[18], (L, D, N_GROUPS), D ** -0.5),
        "router_grp_b": nrm(ks[19], (L, N_GROUPS), 0.01),
        "router_exp_w": nrm(ks[20], (L, D, N_EXPERTS), D ** -0.5),
        "router_exp_b": nrm(ks[21], (L, N_EXPERTS), 0.01),
        "moe_w1": nrm(ks[22], (L, N_EXPERTS, D, D_EXPERT), D ** -0.5),
        "moe_w3": nrm(ks[23], (L, N_EXPERTS, D, D_EXPERT), D ** -0.5),
        "moe_w2": nrm(ks[24], (L, N_EXPERTS, D_EXPERT, D), D_EXPERT ** -0.5),
        "final_g": 1.0 + nrm(ks[25], (D,), 0.02),
    }

def reference(x, norm1_g, w_in, conv_a_w, w_a_out, conv_b_w, conv_b_b, lru_wa, lru_ba,
              lru_wx, lru_bx, lru_lambda, w_b_out, pool_w, pool_scale, w_c_out, w_o,
              norm2_g, router_grp_w, router_grp_b, router_exp_w, router_exp_b,
              moe_w1, moe_w3, moe_w2, final_g):
    for l in range(DEPTH):
        h = rmsnorm(x, norm1_g[l])
        x = x + mixer_sublayer(h, w_in[l], conv_a_w[l], w_a_out[l], conv_b_w[l], conv_b_b[l],
                               lru_wa[l], lru_ba[l], lru_wx[l], lru_bx[l], lru_lambda[l],
                               w_b_out[l], pool_w[l], pool_scale[l], w_c_out[l], w_o[l])
        h = rmsnorm(x, norm2_g[l])
        x = x + hier_moe(h, router_grp_w[l], router_grp_b[l], router_exp_w[l], router_exp_b[l],
                         moe_w1[l], moe_w3[l], moe_w2[l])
    return rmsnorm(x, final_g)


_drawn_inputs = setup_inputs


def setup_inputs(seed=0):
    import zlib

    import numpy as np

    out = dict(_drawn_inputs(seed))
    spreads = {}
    factors = {'lru_ba': 64.0,
     'lru_bx': 64.0,
     'pool_scale': 10.815,
     'router_grp_b': 19.173,
     'router_exp_b': 35.441,
     'final_g': 7.87,
     'conv_b_b': 4.33,
     'norm2_g': 3.691}
    for name, (base, spread) in spreads.items():
        noise = np.random.default_rng([zlib.crc32(name.encode()), seed]).standard_normal(out[name].shape)
        drawn = base * np.exp(spread * noise) if base else spread * noise
        out[name] = __import__('jax').numpy.asarray(drawn.astype(out[name].dtype))
    for name, factor in factors.items():
        out[name] = (out[name] * factor).astype(out[name].dtype)
    return out
```

```python
from contextlib import ExitStack

import concourse.bass as bass
from concourse import mybir

P = 128
SEQ, D = 512, 1024
TT = SEQ // P
KD = D // P
NE, NG, EPG = 16, 4, 4
DE = 512
N = 512
RAW_SLOTS = 6
SUB_SLOTS = 4
EXTRAS = 7
SLOTS = (NE + EXTRAS) * P
WINDOWS = (2, 4, 8, 16)
BIG = 1.0e30
EPS = 1e-6

F32, F32R = mybir.dt.float32, mybir.dt.float32r
F16, I32, U32 = mybir.dt.float16, mybir.dt.int32, mybir.dt.uint32
ALU = mybir.AluOpType
ACT = mybir.ActivationFunctionType
AX_X = mybir.AxisListType.X
MUL, ADD, SUB = ALU.mult, ALU.add, ALU.subtract

JOBS = [
    ("a_c", 512, 4), ("a_x", 1024, 4), ("a_b", 0, 4), ("c_u", 3584, 4),
    ("gate", 4096, 4), ("pool", 0, 1), ("a_out", 0, 2), ("gate", 4608, 4), ("a_out", 1, 2),
    ("b_x0", 1536, 4), ("gate", 6144, 4), ("c_out", 0, 2), ("lru_r0", 0, 1), ("lru_i0", 0, 0),
    ("gate", 6656, 4), ("c_out", 1, 2), ("b_y0", 2560, 4),
    ("b_x1", 2048, 4), ("gate", 5120, 4), ("lru_r1", 1, 1), ("lru_i1", 1, 0), ("b_y1", 3072, 4),
    ("b_out", 0, 4), ("gate", 5632, 4), ("b_out", 1, 4), ("w_o", 0, 4), ("w_o", 1, 4),
]
NJ = len(JOBS)
TITLES = []
for _kind, _arg, _n in JOBS:
    _same = sum(t.rstrip("0123456789") == _kind for t in TITLES)
    TITLES.append(_kind if _kind[-1] in "01" or _kind in ("a_c", "a_x", "a_b", "c_u", "pool") else f"{_kind}{_same}")
JOB = {t: i for i, t in enumerate(TITLES)}

SUBS, CHUNK_OF_JOB = [], []
_c = 0
for _j, (_kind, _arg, _n) in enumerate(JOBS):
    CHUNK_OF_JOB.append(_c)
    for _i in range(_n):
        SUBS.append((_j, _c + _i // 2, _i % 2, _i))
    _c += (_n + 1) // 2
MIX_CHUNKS, MIX_SUBS = _c, len(SUBS)
SUBS_BEFORE = [sum(1 for s in SUBS if s[0] < j) for j in range(NJ + 1)]
assert MIX_SUBS == SUBS_BEFORE[NJ]

ROWS = {}
_r = 0
for _name, _n in (("norm1_g", 8), ("conv_a_w", 12), ("conv_b_w", 32), ("conv_b_b", 8),
                  ("lru_ba", 8), ("lru_bx", 8), ("lru_lambda", 8), ("pool_scale", 4)):
    ROWS[_name] = _r
    _r += _n
NROWS = _r


def trunk(nc, x, norm1_g, w_in, conv_a_w, w_a_out, conv_b_w, conv_b_b, lru_wa, lru_ba, lru_wx,
          lru_bx, lru_lambda, w_b_out, pool_w, pool_scale, w_c_out, w_o, norm2_g, router_grp_w,
          router_grp_b, router_exp_w, router_exp_b, moe_w1, moe_w3, moe_w2, final_g, out):
    x_rows = x.rearrange("b (t p) d -> (b t) p d", p=P)
    out_rows = out.rearrange("b (t p) d -> (b t) p d", p=P)

    def chunks_of(w):
        return w.rearrange("(c k p) (m n) -> c m p k n", p=P, k=4, n=N)

    w_in_c, w_a_c, w_b_c, w_c_c, w_o_c = (chunks_of(w[0]) for w in (w_in, w_a_out, w_b_out, w_c_out, w_o))
    w1_c = moe_w1.rearrange("l e (c k p) n -> (l e) c p k n", p=P, k=4)
    w3_c = moe_w3.rearrange("l e (c k p) n -> (l e) c p k n", p=P, k=4)
    w2_c = moe_w2.rearrange("l e (k p) (c n) -> (l e) c p k n", p=P, n=N)

    h2_dram = nc.dram_tensor("h2_rows", (SEQ, D), F32, kind="Internal").ap()
    y_dram = nc.dram_tensor("expert_rows", (SLOTS, D), F32, kind="Internal").ap()
    y_blocks = y_dram.rearrange("(b p) d -> b p d", p=P)

    with ExitStack() as ctx:
        def sb(name, shape, dt=F32):
            return ctx.enter_context(nc.sbuf_tensor(name, shape, dt))

        def sem(name):
            return ctx.enter_context(nc.semaphore(name))

        ps = ctx.enter_context(nc.psum_tensor("ps", [P, 8, N], F32))

        raw = sb("raw", [P, RAW_SLOTS, 4, N])
        w_hi = sb("w_hi", [P, SUB_SLOTS, 2, N], F32R)
        w_lo = sb("w_lo", [P, SUB_SLOTS, 2, N], F32R)
        h_hi = sb("h_hi", [P, KD, SEQ], F32R)
        h_lo = sb("h_lo", [P, KD, SEQ], F32R)
        y_hi = sb("y_hi", [P, KD, SEQ], F32R)
        y_lo = sb("y_lo", [P, KD, SEQ], F32R)
        m = sb("m", [P, 4 * D])
        sg = sb("sg", [P, 4, SEQ])
        ta = sb("ta", [P, 4, SEQ])
        tb = sb("tb", [P, 4, SEQ])
        tc = sb("tc", [P, 4, SEQ])
        td = sb("td", [P, 4, SEQ])
        ident = sb("ident", [P, P])
        rows = sb("rows", [NROWS, P])
        cols = sb("cols", [P, NROWS])
        c8 = sb("c8", [P, 10, KD])
        inv_cnt = sb("inv_cnt", [P, 4, 16])
        stat = sb("stat", [P, 8, TT])
        ltri = sb("ltri", [P, P], F16)
        ones16 = sb("ones16", [P, P], F16)
        tok_id = sb("tok_id", [P, TT], F16)
        slot_iota = sb("slot_iota", [P, P])
        w_r = sb("w_r", [P, KD, 20])
        b_r = sb("b_r", [P, 20])
        rc = sb("rc", [P, 4, TT, NE])
        r1 = sb("r1", [P, 12, TT])
        routed16 = sb("routed16", [P, TT, NE], F16)
        cnt = sb("cnt", [P, 6, NE])
        pos_i = sb("pos_i", [P, 2, TT], I32)
        pos_rel = sb("pos_rel", [P, 2, TT])
        tick = sb("tick", [P, 1], F16)
        idx = sb("idx", [P, 1], I32)
        xtra = sb("xtra", [1, 8, NE])
        xtra_n = sb("xtra_n", [1, 8])
        xtra_i = sb("xtra_i", [1, 9], I32)

        m_rows = m[:, :].rearrange("p (t d) -> p t d", d=D)
        mt = m[:, :].rearrange("p (k s) -> p k s", s=SEQ)
        flat = {n: t[:, :, :].rearrange("p a b -> p (a b)") for n, t in (("ta", ta), ("tb", tb), ("tc", tc), ("td", td))}
        norm2_row, final_row = flat["tb"][:, 0:D], flat["tb"][:, D:2 * D]
        h2_nat = [flat["td"][:, 0:D], flat["td"][:, D:2 * D]]
        h2_t = [flat["tc"][:, i * D:(i + 1) * D].rearrange("p (k s) -> p k s", s=P) for i in range(2)]
        sel = flat["ta"][:, 0:D]
        hid = flat["ta"][:, D:D + DE]
        silu = flat["ta"][:, D + DE:D + 2 * DE]
        y_out = flat["tc"][:, 0:D]
        y_last = flat["td"][:, 0:D]
        y_got = [[raw[:, t, 2 * k:2 * k + 2, :].rearrange("p a b -> p (a b)") for k in range(2)] for t in range(TT)]
        rt = sg[:, 1:3, :].rearrange("p a (b t e) -> p (a b) t e", t=TT, e=NE)
        logit = sg[:, 3, 0:20 * TT].rearrange("p (t e) -> p t e", e=20)
        ranks = sg[:, 3, P:P + (TT + 1) * NE]
        slot_of = sg[:, 0, :].bitcast(F16).rearrange("p (a s) -> p a s", s=P)

        raw_in = [sem(f"raw_in{i}") for i in range(RAW_SLOTS)]
        hi_made, lo_made, sub_used = sem("hi_made"), sem("lo_made"), sem("sub_used")
        job_done = sem("job_done")
        act_read, dve_read = sem("act_read"), sem("dve_read")
        named = {}

        def s(name):
            if name not in named:
                named[name] = sem(name)
            return named[name]

        reader = {"a_c": "act", "a_x": "dve", "a_b": "dve", "c_u": "act", "gate": "act", "pool": "both",
                  "a_out": "dve", "c_out": "dve", "b_out": "dve", "lru_r0": "act", "lru_i0": "act",
                  "lru_r1": "act", "lru_i1": "act", "b_x0": "both", "b_x1": "both", "b_y0": "act",
                  "b_y1": "act", "w_o": "dve"}

        def act_reads(j):
            return sum(reader[k] in ("act", "both") for k, _, _ in JOBS[:j + 1])

        def dve_reads(j):
            return sum(reader[k] in ("dve", "both") for k, _, _ in JOBS[:j + 1])

        def bank(j, q):
            return 4 * (j % 2) + q

        def col(name, i):
            r = ROWS[name] + i
            return cols[:, r:r + 1]

        def mix_sub(i):
            j, c, half, _ = SUBS[i]
            t = raw[:, c % RAW_SLOTS, 2 * half:2 * half + 2, :]
            if JOBS[j][0] == "pool":
                return raw[:, c % RAW_SLOTS, 0:1, :], 1
            return t, 2

        block = ctx.enter_context(nc.Block())

        def body_base(e):
            return (MIX_CHUNKS, MIX_SUBS, 0) if isinstance(e, int) and e == 0 else (MIX_CHUNKS + 4, MIX_SUBS + 8, e - 1)

        XTRA_BASE = (MIX_CHUNKS + 6 * NE, MIX_SUBS + 12 * NE)

        @block.sync
        def _(sp):
            def load(c0, turn, dst, src, subs_before):
                slot = c0 % RAW_SLOTS
                if subs_before is not None:
                    sp.wait_ge(lo_made, subs_before)
                sp.dma_start(dst, src).then_inc(raw_in[slot], 16)

            def chunk_end(c):
                if c < MIX_CHUNKS:
                    return sum(1 for q in SUBS if q[1] <= c)
                return MIX_SUBS + 2 * (c - MIX_CHUNKS + 1)

            for t in range(TT):
                sp.dma_start(m_rows[:, t, :], x_rows[t]).then_inc(s(f"x_in{t}"), 16)
            for j, (kind, arg, n) in enumerate(JOBS):
                for i in range((n + 1) // 2):
                    c = CHUNK_OF_JOB[j] + i
                    slot = c % RAW_SLOTS
                    free = chunk_end(c - RAW_SLOTS) if c >= RAW_SLOTS else None
                    dst = raw[:, slot, :, :]
                    if kind in ("lru_r0", "lru_r1"):
                        h = slice(4 * arg, 4 * arg + 4)
                        if free is not None:
                            sp.wait_ge(lo_made, free)
                        for a, w in enumerate((lru_wa, lru_wx)):
                            sp.dma_start(raw[:, slot, a, :].rearrange("p (h j) -> p h j", j=P),
                                         w[0, h].rearrange("h i j -> i h j")).then_inc(s(f"lru_in{arg}"), 16)
                        sp.sem_inc(raw_in[slot], 16)
                        continue
                    if kind == "pool":
                        if free is not None:
                            sp.wait_ge(lo_made, free)
                        sp.dma_start(raw[:, slot, 0, :].rearrange("p (h j) -> p h j", j=P),
                                     pool_w[0].rearrange("h i j -> i h j")).then_inc(raw_in[slot], 16)
                        continue
                    if kind in ("a_out", "b_out", "c_out"):
                        src = {"a_out": w_a_c, "b_out": w_b_c, "c_out": w_c_c}[kind][i, arg]
                    elif kind == "w_o":
                        src = w_o_c[i, arg]
                    else:
                        src = w_in_c[i, arg // N]
                    load(c, 0, dst, src, free)

            def expert_chunk(c0, turn, src):
                load(c0, turn, raw[:, c0 % RAW_SLOTS, :, :], src,
                     12 * turn + chunk_end(c0 - RAW_SLOTS))

            for i, w in enumerate((w1_c, w1_c, w3_c, w3_c)):
                expert_chunk(MIX_CHUNKS + i, 0, w[0, i % 2])

            def body(e, last=False):
                c0 = MIX_CHUNKS + 4
                turn = e - 1
                if not last:
                    for i, w in enumerate((w1_c, w1_c, w3_c, w3_c)):
                        expert_chunk(c0 + i, turn, w[e, i % 2])
                for i in range(2):
                    expert_chunk(c0 + (i if last else 4 + i), turn, w2_c[e - 1, i])

            with sp.Fori(1, NE) as e:
                body(e)
            body(NE, last=True)

            sp.wait_ge(s("extras_known"), 1)
            n_extra = sp.value_load(xtra_i[0:1, 8:9], min_val=0, max_val=EXTRAS)
            with sp.If(n_extra > 0):
                with sp.Fori(0, EXTRAS) as j:
                    with sp.If(n_extra > j):
                        e = sp.value_load(xtra_i[0:1, bass.ds(j, 1)], min_val=0, max_val=NE - 1)
                        c0 = XTRA_BASE[0]
                        for i, w in enumerate((w1_c, w1_c, w3_c, w3_c, w2_c, w2_c)):
                            expert_chunk(c0 + i, j, w[e, i % 2])

            for t in range(TT):
                sp.wait_ge(s("final_rows"), t + 1)
                sp.dma_start(out_rows[t], y_got[t][0]).then_inc(s(f"stored{t}"), 16)
            for t in range(TT):
                sp.wait_ge(s(f"stored{t}"), 16)

        @block.gpsimd
        def _(pool):
            nc.gpsimd.memset(ident[:, :], 0.0).then_inc(s("pool_step"), 1)
            pool.wait_ge(s("pool_step"), 1)
            nc.gpsimd.affine_select(out=ident[:, :], in_=ident[:, :], compare_op=ALU.not_equal, fill=1.0, base=0,
                                    pattern=[[-1, P]], channel_multiplier=1).then_inc(s("ident_made"), 1)
            pool.dma_start(w_r[:, :, 0:NG], router_grp_w[0].rearrange("(k p) g -> p k g", p=P)).then_inc(s("router_in"), 16)
            pool.dma_start(w_r[:, :, NG:20], router_exp_w[0].rearrange("(k p) g -> p k g", p=P)).then_inc(s("router_in"), 16)
            pool.dma_start(b_r[:, 0:NG], router_grp_b.partition_broadcast(P)).then_inc(s("router_in"), 16)
            pool.dma_start(b_r[:, NG:20], router_exp_b.partition_broadcast(P)).then_inc(s("router_in"), 16)
            nc.gpsimd.iota(slot_iota[:, :], pattern=[[1, P]], base=0, channel_multiplier=0,
                           allow_small_or_imprecise_dtypes=True).then_inc(s("iotas"), 1)
            nc.gpsimd.iota(tok_id[:, :], pattern=[[P, TT]], base=0, channel_multiplier=1,
                           allow_small_or_imprecise_dtypes=True).then_inc(s("iotas"), 1)
            nc.gpsimd.iota(rc[:, 0, :, :], pattern=[[0, TT], [1, NE]], base=-32, channel_multiplier=0,
                           allow_small_or_imprecise_dtypes=True).then_inc(s("iotas"), 1)
            nc.gpsimd.iota(rc[:, 1, :, :].rearrange("p t (g e) -> p t g e", e=EPG), pattern=[[0, TT], [1, NG], [0, EPG]],
                           base=-8, channel_multiplier=0, allow_small_or_imprecise_dtypes=True).then_inc(s("iotas"), 1)
            nc.gpsimd.iota(rc[:, 2, :, 0:NG], pattern=[[0, TT], [1, NG]], base=-8, channel_multiplier=0,
                           allow_small_or_imprecise_dtypes=True).then_inc(s("iotas"), 1)
            nc.gpsimd.iota(rc[:, 3, :, :], pattern=[[0, TT], [P, NE]], base=0, channel_multiplier=0,
                           allow_small_or_imprecise_dtypes=True).then_inc(s("iotas"), 1)
            nc.gpsimd.iota(cnt[:, 0, :], pattern=[[-P, NE]], base=(NE - 1) * P, channel_multiplier=0,
                           allow_small_or_imprecise_dtypes=True).then_inc(s("iotas"), 1)
            nc.gpsimd.iota(xtra[:, :, :], pattern=[[1, 8], [0, NE]], base=0, channel_multiplier=0,
                           allow_small_or_imprecise_dtypes=True).then_inc(s("iotas"), 1)
            nc.gpsimd.iota(inv_cnt[:, :, :], pattern=[[0, 4], [1, 16]], base=1, channel_multiplier=0,
                           allow_small_or_imprecise_dtypes=True).then_inc(s("iotas"), 1)
            nc.gpsimd.memset(ones16[:, :], 1.0).then_inc(s("pool_step"), 1)
            pool.wait_ge(s("pool_step"), 2)
            nc.gpsimd.affine_select(out=ltri[:, :], in_=ones16[:, :], compare_op=ALU.is_gt, fill=0.0, base=0,
                                    pattern=[[1, P]], channel_multiplier=-1).then_inc(s("iotas"), 1)

            flat_x = x.rearrange("b t d -> (b t) d")
            pool.wait_ge(s("y_a"), 4)
            for at in range(NE * P, SLOTS, SEQ):
                n_rows = min(SEQ, SLOTS - at)
                pool.dma_start(y_dram[at:at + n_rows, :], flat_x[0:n_rows, :]).then_inc(s(f"filled{at}"), 16)
            for at in range(NE * P, SLOTS, SEQ):
                pool.wait_ge(s(f"filled{at}"), 16)

            pool.wait_ge(s("y_b1_scan"), 4)
            pool.dma_start(norm2_row, norm2_g.partition_broadcast(P)).then_inc(s("norm_rows"), 16)
            pool.dma_start(final_row, final_g.rearrange("(l d) -> l d", l=1).partition_broadcast(P)).then_inc(s("norm_rows"), 16)
            pool.wait_ge(s("m_split"), 2)
            pool.dma_start(m_rows, x_rows.rearrange("t p d -> p t d")).then_inc(s("x_again"), 16)
            for t in range(TT):
                pool.wait_ge(s("h2"), t + 1)
                pool.dma_start(h2_dram[t * P:(t + 1) * P, :], h2_nat[t % 2]).then_inc(s(f"h2_out{t}"), 16)
            for t in range(TT):
                pool.wait_ge(s(f"h2_out{t}"), 16)

            def carry_waits(n):
                if not (isinstance(n, int) and n == 0):
                    pool.wait_ge(s("ticks"), n)
                nc.gpsimd.tensor_tensor(tick[:, :], ones16[:, 0:1], ones16[:, 0:1], MUL).then_inc(s("ticks"), 1)

            def gather(b, tick_no, first=False):
                pool.wait_ge(s("idx_made"), b + 1)
                if not first:
                    pool.wait_ge(s("sel_turned"), b)
                carry_waits(tick_no)
                nc.gpsimd.indirect_dma_start(out=sel, out_offset=None, in_=h2_dram[:, :],
                                             in_offset=bass.IndirectOffsetOnAxis(ap=idx[:, 0:1], axis=0)
                                             ).then_inc(s("sel_in"), 16)

            def store(b, tick_no, rows_of=None):
                pool.wait_ge(s("y_act"), b + 1)
                pool.wait_ge(s("y_dve"), b + 1)
                carry_waits(tick_no)
                pool.dma_start(y_blocks[b], y_out if rows_of is None else rows_of).then_inc(s("y_stored"), 16)

            gather(0, 0, first=True)
            gather(1, 1)
            gather(2, 2)
            with pool.Fori(1, NE - 2) as e:
                gather(e + 2, 2 * e + 1)
                store(e - 1, 2 * e + 2)
            store(NE - 3, 2 * NE - 3)
            store(NE - 2, 2 * NE - 2)
            store(NE - 1, 2 * NE - 1, y_last)
            pool.wait_ge(s("y_stored"), 16 * NE)

            pool.wait_ge(s("extras_known"), 1)
            n_extra = pool.value_load(xtra_i[0:1, 8:9], min_val=0, max_val=EXTRAS)
            with pool.If(n_extra > 0):
                with pool.Fori(0, EXTRAS) as j:
                    with pool.If(n_extra > j):
                        gather(NE + j, 2 * (NE + j))
                        store(NE + j, 2 * (NE + j) + 1)
                        pool.wait_ge(s("y_stored"), 16 * (NE + 1 + j))

            for t in range(TT):
                for k in range(2):
                    nc.gpsimd.indirect_dma_start(out=y_got[t][k], out_offset=None, in_=y_dram[:, :],
                                                 in_offset=bass.IndirectOffsetOnAxis(ap=pos_i[:, k, t:t + 1], axis=0)
                                                 ).then_inc(s(f"y_got{t}{k}"), 16)

        @block.scalar
        def _(act):
            made = [0]

            def hi_sub(dst_slot, src, cols_n):
                nc.scalar.activation(w_hi[:, dst_slot, 0:cols_n, :], src, ACT.Copy).then_inc(hi_made, 1)

            def split_next():
                i = made[0]
                j, c, half, _ = SUBS[i]
                if JOBS[j][0].startswith("lru"):
                    act.wait_ge(s(f"lru_in{JOBS[j][1]}"), 32)
                act.wait_ge(raw_in[c % RAW_SLOTS], 16 * (c // RAW_SLOTS + 1))
                if i >= SUB_SLOTS:
                    act.wait_ge(sub_used, i - SUB_SLOTS + 1)
                t, n = mix_sub(i)
                hi_sub(i % SUB_SLOTS, t, n)
                made[0] += 1

            def split_to(j):
                while made[0] < SUBS_BEFORE[min(j + 1, NJ)]:
                    split_next()

            def more(j):
                if made[0] < SUBS_BEFORE[min(j + 3, NJ)]:
                    split_next()

            def moe_hi(i0, turn, c0, k):
                c = c0 + k // 2
                act.wait_ge(raw_in[c % RAW_SLOTS], 16 * (turn + c // RAW_SLOTS + 1))
                act.wait_ge(sub_used, 12 * turn + (i0 + k - SUB_SLOTS + 1))
                hi_sub((i0 + k) % SUB_SLOTS, raw[:, c % RAW_SLOTS, 2 * (k % 2):2 * (k % 2) + 2, :], 2)

            for name, w, k in (("norm1_g", norm1_g, 8), ("conv_a_w", conv_a_w, 12), ("conv_b_w", conv_b_w, 32),
                               ("conv_b_b", conv_b_b, 8), ("lru_ba", lru_ba, 8), ("lru_bx", lru_bx, 8),
                               ("lru_lambda", lru_lambda, 8), ("pool_scale", pool_scale, 4)):
                src = w if len(w.shape) == 2 else w.rearrange("l a c -> l (a c)")
                act.dma_start(rows[ROWS[name]:ROWS[name] + k, :],
                               src.rearrange("l (r c) -> (l r) c", c=P)).then_inc(s("rows_in"), 16)
            for t in (0, 2):
                act.wait_ge(s(f"x_in{t}"), 16)
                nc.scalar.activation(flat["ta"][:, t // 2 * D:(t // 2 + 1) * D], m_rows[:, t, :],
                                     ACT.Square, accum_out=stat[:, 0, t:t + 1]).then_inc(s("sq1"), 1)
            act.wait_ge(s("ms1"), 1)
            nc.scalar.activation(stat[:, 2, :], stat[:, 1, :], ACT.Sqrt).then_inc(s("root1"), 1)
            act.wait_ge(s("rstd1"), 1)
            for t in (1, 3):
                nc.scalar.activation(m_rows[:, t, :], m_rows[:, t, :], ACT.Copy, scale=stat[:, 3, t:t + 1]).then_inc(s(f"x_scaled{t}"), 1)
            split_next()
            split_next()
            for k in range(KD):
                if k == 4 or k == 6:
                    split_next()
                act.wait_ge(s("x_turned"), k + 1)
                nc.scalar.activation(h_hi[:, k, :], ps[:, k, :], ACT.Identity, scale=col("norm1_g", k)).then_inc(s("h_hi"), 1)
            act.wait_ge(s("cols_made"), 1)
            lam = cols[:, ROWS["lru_lambda"]:ROWS["lru_lambda"] + KD]
            nc.scalar.activation(c8[:, 0, :], lam, ACT.Abs).then_inc(s("abs_lam"), 1)
            act.wait_ge(s("abs_lam"), 1)
            nc.scalar.activation(c8[:, 1, :], c8[:, 0, :], ACT.Exp, scale=-1.0).then_inc(s("exp_lam"), 1)

            def wait_job(j):
                act.wait_ge(job_done, j + 1)

            def hi_of(src, name_in, name_out, y0, src_wait=None):
                for q in range(4):
                    act.wait_ge(s(name_in), q + 1)
                    nc.scalar.activation(y_hi[:, y0 + q, :], src[:, q, :], ACT.Copy).then_inc(s(name_out), 1)

            for j, (kind, arg, n) in enumerate(JOBS):
                title = TITLES[j]
                split_to(j + 1)
                if kind == "a_c":
                    wait_job(j)
                    for q in range(4):
                        ins = nc.scalar.activation(tb[:, q, :], ps[:, bank(j, q), :], ACT.Copy).then_inc(s("a_c"), 1)
                    act.wait_ge(s("a_c"), 4)
                    act.sem_inc(act_read, 1)
                elif kind == "a_b":
                    hi_of(ta, "y_a", "y_a_hi", 0)
                elif kind == "c_u":
                    wait_job(j)
                    act.wait_ge(s("a_u"), 4)
                    for q in range(4):
                        nc.scalar.activation(tb[:, q, :], ps[:, bank(j, q), :], ACT.Copy).then_inc(s("c_u"), 1)
                    act.wait_ge(s("c_u"), 4)
                    act.sem_inc(act_read, 1)
                    hi_of(td, "pooled", "pooled_hi", 4)
                elif kind == "gate":
                    g = int(title[4:])
                    wait_job(j)
                    if g:
                        act.wait_ge(s("gated"), 4 * g)
                    for q in range(4):
                        nc.scalar.activation(sg[:, q, :], ps[:, bank(j, q), :], ACT.Sigmoid).then_inc(s("gate"), 1)
                    act.wait_ge(s("gate"), 4 * g + 4)
                    act.sem_inc(act_read, 1)
                elif kind == "pool":
                    wait_job(j)
                    for q in range(4):
                        nc.scalar.activation(y_hi[:, 4 + q, :], ps[:, bank(j, q), :], ACT.Identity,
                                             scale=col("pool_scale", q)).then_inc(s("y_c_hi"), 1)
                    act.wait_ge(s("y_c_hi"), 4)
                    act.sem_inc(act_read, 1)
                elif kind in ("b_x0", "b_x1"):
                    g = arg // N - 3
                    wait_job(j)
                    if g == 0:
                        act.wait_ge(s("y_a_lo"), 4)
                    else:
                        act.wait_ge(s("y_b0_prod"), 4)
                    for q in range(4):
                        c = 4 * g + q
                        nc.scalar.activation(ta[:, q, :], ps[:, bank(j, q), :], ACT.Identity,
                                             scale=col("conv_b_w", 3 * KD + c), bias=col("conv_b_b", c)).then_inc(s(f"x_b{g}_tap"), 1)
                    act.wait_ge(s(f"x_b{g}_tap"), 4)
                    act.sem_inc(act_read, 1)
                    hi_of(ta, f"x_b{g}", f"x_b{g}_hi", 4 * g)
                elif kind in ("lru_r0", "lru_r1"):
                    g = arg
                    wait_job(j)
                    act.wait_ge(s("pooled"), 4)
                    if g == 1:
                        act.wait_ge(s("y_b0_prod"), 4)
                    for q in range(4):
                        nc.scalar.activation(tb[:, q, :], ps[:, bank(j, q), :], ACT.Sigmoid,
                                             bias=col("lru_ba", 4 * g + q)).then_inc(s(f"r{g}"), 1)
                    act.wait_ge(s(f"r{g}"), 4)
                    act.sem_inc(act_read, 1)
                elif kind in ("lru_i0", "lru_i1"):
                    g = arg
                    wait_job(j)
                    for q in range(4):
                        nc.scalar.activation(tc[:, q, :], ps[:, bank(j, q), :], ACT.Sigmoid,
                                             bias=col("lru_bx", 4 * g + q)).then_inc(s(f"i{g}"), 1)
                    act.wait_ge(s(f"i{g}"), 4)
                    act.sem_inc(act_read, 1)
                    more(j)
                    act.wait_ge(s("c8_made"), 1)
                    if g == 0:
                        act.wait_ge(s("pooled_lo"), 4)
                    else:
                        act.wait_ge(s("y_b0_lo"), 4)
                    for q in range(4):
                        nc.scalar.activation(td[:, q, :], tb[:, q, :], ACT.Tanh,
                                             scale=c8[:, 8, 4 * g + q:4 * g + q + 1]).then_inc(s(f"t{g}"), 1)
                    more(j)
                    for q in range(4):
                        act.wait_ge(s(f"t{g}"), q + 1)
                        nc.scalar.activation(tb[:, q, :], tb[:, q, :], ACT.Exp,
                                             scale=c8[:, 9, 4 * g + q:4 * g + q + 1]).then_inc(s(f"a{g}"), 1)
                    more(j)
                    for q in range(4):
                        act.wait_ge(s(f"ratio{g}"), q + 1)
                        nc.scalar.activation(td[:, q, :], td[:, q, :], ACT.Sqrt, scale=2.0).then_inc(s(f"root_b{g}"), 1)
                elif kind in ("b_y0", "b_y1"):
                    g = arg // N - 5
                    wait_job(j)
                    act.wait_ge(s(f"ratio{g}"), 4)
                    for q in range(4):
                        nc.scalar.activation(ta[:, q, :], ps[:, bank(j, q), :], ACT.Gelu_apprx_tanh).then_inc(s(f"gelu{g}"), 1)
                    act.wait_ge(s(f"gelu{g}"), 4)
                    act.sem_inc(act_read, 1)
                    more(j)
                    hi_of(td, f"y_b{g}_prod", f"y_b{g}_hi", 4 * g)
                elif kind == "b_out":
                    act.wait_ge(job_done, JOB["gate5"] + 1)
                    for q in range(4):
                        act.wait_ge(s("m_sum"), 4 * arg + q + 1)
                        nc.scalar.activation(h_hi[:, 4 * arg + q, :], mt[:, 4 * arg + q, :], ACT.Copy).then_inc(s("m_hi"), 1)

            def root_of(t):
                act.wait_ge(s("x_mid"), t + 1)
                if t:
                    act.wait_ge(s("sq2"), t)
                nc.scalar.activation(flat["ta"][:, 0:D], m_rows[:, t, :], ACT.Square,
                                     accum_out=stat[:, 0, t:t + 1]).then_inc(s("sq2"), 1)
                act.wait_ge(s("ms2"), t + 1)
                nc.scalar.activation(stat[:, 2, t:t + 1], stat[:, 1, t:t + 1], ACT.Sqrt).then_inc(s("root2"), 1)

            def copy_h2_t(t):
                act.wait_ge(s("h2_turned"), t + 1)
                if t >= 2:
                    act.wait_ge(s("logits"), t - 1)
                b0 = bank(JOB["w_o0"], 2 * (t % 2))
                nc.scalar.activation(h2_t[t % 2].rearrange("p k s -> p (k s)"),
                                     ps[:, b0:b0 + 2, :].rearrange("p a b -> p (a b)"), ACT.Copy).then_inc(s("h2_t"), 1)

            c0, i0 = MIX_CHUNKS, MIX_SUBS
            root_of(0)
            root_of(1)
            copy_h2_t(0)
            root_of(2)
            copy_h2_t(1)
            root_of(3)
            copy_h2_t(2)
            for k in range(2):
                moe_hi(i0, 0, c0, k)
            copy_h2_t(3)
            for k in range(2, 4):
                moe_hi(i0, 0, c0, k)
            act.wait_ge(s("soft_in"), 1)
            nc.scalar.activation(rt[:, 14, :, 0:NG], rt[:, 13, :, 0:NG], ACT.Exp).then_inc(s("soft_exp"), 1)
            nc.scalar.activation(r1[:, 6, :], r1[:, 5, :], ACT.Exp).then_inc(s("soft_exp"), 1)

            def sel_hi(b):
                act.wait_ge(s("sel_turned"), b + 1)
                nc.scalar.activation(h_hi[:, :, 0:P], ps[:, 4:6, :].rearrange("p a (k s) -> p (a k) s", s=P),
                                     ACT.Copy).then_inc(s("sel_hi"), 1)

            def silu_of(b, first=False):
                act.wait_ge(s("h1"), b + 1)
                if not first:
                    act.wait_ge(s("hid"), b)
                nc.scalar.activation(silu, ps[:, 0, :], ACT.Silu).then_inc(s("silu"), 1)

            def hid_hi(b):
                act.wait_ge(s("hid_turned"), b + 1)
                nc.scalar.activation(h_hi[:, 0:4, P:2 * P], ps[:, 6, :].rearrange("p (k s) -> p k s", s=P),
                                     ACT.Copy).then_inc(s("hid_hi"), 1)

            def y_half(b, first=False, last=False):
                act.wait_ge(s("y"), b + 1)
                if not first and not last:
                    act.wait_ge(s("y_stored"), 16 * b)
                nc.scalar.activation((y_last if last else y_out)[:, 0:N], ps[:, 2, :], ACT.Copy).then_inc(s("y_act"), 1)

            sel_hi(0)
            for k in range(4, 8):
                moe_hi(i0, 0, c0, k)
            silu_of(0, first=True)
            sel_hi(1)
            c1, i1 = MIX_CHUNKS + 4, MIX_SUBS + 8
            for k in range(4):
                moe_hi(i1, 0, c1, k)

            def body(e, turn_next=True, first=False):
                turn = e - 1
                for k in range(4, 8):
                    moe_hi(i1, turn, c1, k)
                silu_of(e)
                hid_hi(e - 1)
                for k in range(8, 12):
                    moe_hi(i1, turn, c1, k)
                if turn_next:
                    sel_hi(e + 1)
                for k in range(4):
                    moe_hi(i1, e, c1, k)
                y_half(e - 1, first)

            body(1, first=True)
            with act.Fori(2, NE - 1) as e:
                body(e)
            body(NE - 1, turn_next=False)
            hid_hi(NE - 1)
            y_half(NE - 1, last=True)

            act.wait_ge(s("extras_known"), 1)
            n_extra = act.value_load(xtra_i[0:1, 8:9], min_val=0, max_val=EXTRAS)
            with act.If(n_extra > 0):
                with act.Fori(0, EXTRAS) as j:
                    with act.If(n_extra > j):
                        b = NE + j
                        cx, ix = XTRA_BASE
                        sel_hi(b)
                        for k in range(8):
                            moe_hi(ix, j, cx, k)
                        silu_of(b)
                        for k in range(8, 12):
                            moe_hi(ix, j, cx, k)
                        hid_hi(b)
                        y_half(b)

            for t in range(TT):
                act.wait_ge(s("merged"), t + 1)
                if t:
                    act.wait_ge(s("sq3"), t)
                nc.scalar.activation(flat["tb"][:, 0:D], m_rows[:, t, :], ACT.Square,
                                     accum_out=stat[:, 4, t:t + 1]).then_inc(s("sq3"), 1)
                act.wait_ge(s("ms3"), t + 1)
                nc.scalar.activation(stat[:, 6, t:t + 1], stat[:, 5, t:t + 1], ACT.Sqrt).then_inc(s("root3"), 1)

        @block.vector
        def _(dve):
            made = [0]
            steps = [0]
            V = nc.vector

            def link(ins):
                steps[0] += 1
                ins.then_inc(s("dve_step"), 1)
                dve.wait_ge(s("dve_step"), steps[0])

            def lo_sub(slot, src, n):
                V.tensor_tensor(w_lo[:, slot, 0:n, :], src, w_hi[:, slot, 0:n, :], SUB).then_inc(lo_made, 1)

            def split_next():
                i = made[0]
                dve.wait_ge(hi_made, i + 1)
                t, n = mix_sub(i)
                lo_sub(i % SUB_SLOTS, t, n)
                made[0] += 1

            def split_to(j):
                while made[0] < SUBS_BEFORE[min(j + 1, NJ)]:
                    split_next()

            def more(j):
                if made[0] < SUBS_BEFORE[min(j + 3, NJ)]:
                    split_next()

            def moe_lo(i0, turn, c0, k):
                dve.wait_ge(hi_made, 12 * turn + (i0 + k + 1))
                c = c0 + k // 2
                lo_sub((i0 + k) % SUB_SLOTS, raw[:, c % RAW_SLOTS, 2 * (k % 2):2 * (k % 2) + 2, :], 2)

            for t in (1, 3):
                dve.wait_ge(s(f"x_in{t}"), 16)
                V.tensor_tensor_reduce(out=flat["tb"][:, t // 2 * D:(t // 2 + 1) * D], in0=m_rows[:, t, :], in1=m_rows[:, t, :],
                                       scale=1.0, scalar=0.0, op0=MUL, op1=ADD,
                                       accum_out=stat[:, 0, t:t + 1]).then_inc(s("sq1"), 1)
            dve.wait_ge(s("sq1"), TT)
            V.tensor_scalar(stat[:, 1, :], stat[:, 0, :], 1.0 / D, EPS, MUL, ADD).then_inc(s("ms1"), 1)
            dve.wait_ge(s("root1"), 1)
            V.reciprocal(stat[:, 3, :], stat[:, 2, :]).then_inc(s("rstd1"), 1)
            dve.wait_ge(s("rstd1"), 1)
            for t in (0, 2):
                V.tensor_scalar(m_rows[:, t, :], m_rows[:, t, :], stat[:, 3, t:t + 1], None, MUL).then_inc(s(f"x_scaled{t}"), 1)
            dve.wait_ge(s("rows_turned"), 1)
            V.tensor_copy(cols[:, :], ps[:, 7, 0:NROWS]).then_inc(s("cols_made"), 1)
            split_next()
            split_next()
            for k in range(KD):
                if k == 4 or k == 6:
                    split_next()
                dve.wait_ge(s("h_hi"), k + 1)
                V.scalar_tensor_tensor(out=h_lo[:, k, :], in0=ps[:, k, :], scalar=col("norm1_g", k),
                                       in1=h_hi[:, k, :], op0=MUL, op1=SUB).then_inc(s("h_lo"), 1)
            dve.wait_ge(s("iotas"), 10)
            for g, w in enumerate(WINDOWS):
                link(V.tensor_scalar(inv_cnt[:, g, :], inv_cnt[:, g, :], float(w), None, ALU.min))
            link(V.reciprocal(inv_cnt[:, :, :], inv_cnt[:, :, :]))
            dve.wait_ge(s("exp_lam"), 1)
            lam = cols[:, ROWS["lru_lambda"]:ROWS["lru_lambda"] + KD]
            e_, z, z2, q_ = c8[:, 1, :], c8[:, 2, :], c8[:, 3, :], c8[:, 4, :]
            link(V.tensor_scalar(z, e_, 2.0, None, ADD))
            link(V.reciprocal(z, z))
            link(V.tensor_tensor(z, z, e_, MUL))
            link(V.tensor_tensor(z2, z, z, MUL))
            link(V.tensor_scalar(q_, z2, 1.0 / 17, None, MUL))
            for d in (15, 13, 11, 9, 7, 5, 3):
                link(V.scalar_tensor_tensor(out=q_, in0=q_, scalar=1.0 / d, in1=z2, op0=ADD, op1=MUL))
            link(V.scalar_tensor_tensor(out=q_, in0=q_, scalar=1.0, in1=z, op0=ADD, op1=MUL))
            link(V.tensor_scalar(c8[:, 5, :], lam, -1.0, 0.0, MUL, ALU.max))
            link(V.scalar_tensor_tensor(out=c8[:, 6, :], in0=q_, scalar=2.0, in1=c8[:, 5, :], op0=MUL, op1=ADD))
            link(V.tensor_scalar(c8[:, 8, :], c8[:, 6, :], 8.0, None, MUL))
            V.tensor_scalar(c8[:, 9, :], c8[:, 6, :], -8.0, None, MUL).then_inc(s("c8_made"), 1)

            def wait_job(j):
                dve.wait_ge(job_done, j + 1)

            def lo_of(src, name_hi, name_out, y0):
                for q in range(4):
                    dve.wait_ge(s(name_hi), q + 1)
                    V.tensor_tensor(y_lo[:, y0 + q, :], src[:, q, :], y_hi[:, y0 + q, :], SUB).then_inc(s(name_out), 1)

            for j, (kind, arg, n) in enumerate(JOBS):
                split_to(j + 1)
                title = TITLES[j]
                if kind == "a_x":
                    wait_job(j)
                    for q in range(4):
                        dve.wait_ge(s("a_c"), q + 1)
                        V.tensor_tensor(tc[:, q, :], ps[:, bank(j, q), :], tb[:, q, :], MUL).then_inc(s("a_u"), 1)
                    dve.wait_ge(s("a_u"), 4)
                    dve.sem_inc(dve_read, 1)
                    for q in range(4):
                        V.tensor_scalar(td[:, q, :], tc[:, q, :], col("conv_a_w", 8 + q), None, MUL).then_inc(s("conv_a"), 1)
                    for tap in (1, 2):
                        more(j)
                        for q in range(4):
                            dve.wait_ge(s("conv_a"), 4 * (tap - 1) + q + 1)
                            V.scalar_tensor_tensor(out=td[:, q, tap:], in0=tc[:, q, 0:SEQ - tap],
                                                   scalar=col("conv_a_w", 4 * (2 - tap) + q), in1=td[:, q, tap:],
                                                   op0=MUL, op1=ADD).then_inc(s("conv_a"), 1)
                elif kind == "a_b":
                    wait_job(j)
                    dve.wait_ge(s("conv_a"), 12)
                    for q in range(4):
                        V.tensor_tensor(ta[:, q, :], ps[:, bank(j, q), :], td[:, q, :], MUL).then_inc(s("y_a"), 1)
                    dve.wait_ge(s("y_a"), 4)
                    dve.sem_inc(dve_read, 1)
                    lo_of(ta, "y_a_hi", "y_a_lo", 0)
                elif kind == "c_u":
                    dve.wait_ge(s("c_u"), 4)
                    for q, w in enumerate(WINDOWS):
                        src, step = tb, 1
                        for lv in range(q + 1):
                            dst = (td, tc)[(q - lv) % 2]
                            V.tensor_copy(dst[:, q, 0:step], src[:, q, 0:step])
                            link(V.tensor_tensor(dst[:, q, step:], src[:, q, step:], src[:, q, 0:SEQ - step], ADD))
                            src, step = dst, 2 * step
                        link(V.tensor_tensor(tc[:, q, 0:16], td[:, q, 0:16], inv_cnt[:, q, :], MUL))
                        link(V.scalar_tensor_tensor(out=td[:, q, 16:], in0=td[:, q, 16:], scalar=1.0 / w, in1=tb[:, q, 16:],
                                                    op0=MUL, op1=SUB))
                        V.tensor_tensor(td[:, q, 0:16], tc[:, q, 0:16], tb[:, q, 0:16], SUB).then_inc(s("pooled"), 1)
                    lo_of(td, "pooled_hi", "pooled_lo", 4)
                elif kind == "pool":
                    wait_job(j)
                    for q in range(4):
                        dve.wait_ge(s("y_c_hi"), q + 1)
                        V.scalar_tensor_tensor(out=y_lo[:, 4 + q, :], in0=ps[:, bank(j, q), :], scalar=col("pool_scale", q),
                                               in1=y_hi[:, 4 + q, :], op0=MUL, op1=SUB).then_inc(s("y_c_lo"), 1)
                    dve.wait_ge(s("y_c_lo"), 4)
                    dve.sem_inc(dve_read, 1)
                elif kind in ("a_out", "c_out", "b_out"):
                    wait_job(j)
                    g = [t for t in TITLES if "_out" in t].index(title)
                    dve.wait_ge(s("gate"), 4 * g + 4)
                    for q in range(4):
                        o = mt[:, 4 * arg + q, :]
                        if kind == "a_out":
                            V.tensor_tensor(o, ps[:, bank(j, q), :], sg[:, q, :], MUL).then_inc(s("gated"), 1)
                        else:
                            V.tensor_tensor(sg[:, q, :], ps[:, bank(j, q), :], sg[:, q, :], MUL).then_inc(s("gate_prod"), 1)
                    if kind == "a_out":
                        dve.wait_ge(s("gated"), 4 * g + 4)
                        dve.sem_inc(dve_read, 1)
                    else:
                        base = 4 * (g - 2)
                        dve.wait_ge(s("gate_prod"), base + 4)
                        dve.sem_inc(dve_read, 1)
                        for q in range(4):
                            o = mt[:, 4 * arg + q, :]
                            ins = V.tensor_tensor(o, o, sg[:, q, :], ADD)
                            ins.then_inc(s("gated"), 1)
                            if kind == "b_out":
                                dve.wait_ge(s("gated"), 4 * g + q + 1)
                                dve.sem_inc(s("m_sum"), 1)
                    if kind == "b_out":
                        for q in range(4):
                            k = 4 * arg + q
                            dve.wait_ge(s("m_hi"), k + 1)
                            V.tensor_tensor(h_lo[:, k, :], mt[:, k, :], h_hi[:, k, :], SUB).then_inc(s("m_lo"), 1)
                        dve.wait_ge(s("m_lo"), 4 * arg + 4)
                        dve.sem_inc(s("m_split"), 1)
                elif kind in ("b_x0", "b_x1"):
                    g = arg // N - 3
                    wait_job(j)
                    for tap in (1, 2, 3):
                        for q in range(4):
                            c = 4 * g + q
                            if tap == 1:
                                dve.wait_ge(s(f"x_b{g}_tap"), q + 1)
                            else:
                                dve.wait_ge(s(f"x_b{g}_sum"), 4 * (tap - 2) + q + 1)
                            ins = V.scalar_tensor_tensor(out=ta[:, q, tap:], in0=ps[:, bank(j, q), 0:SEQ - tap],
                                                         scalar=col("conv_b_w", (3 - tap) * KD + c), in1=ta[:, q, tap:],
                                                         op0=MUL, op1=ADD)
                            ins.then_inc(s(f"x_b{g}") if tap == 3 else s(f"x_b{g}_sum"), 1)
                    dve.wait_ge(s(f"x_b{g}"), 4)
                    dve.sem_inc(dve_read, 1)
                    lo_of(ta, f"x_b{g}_hi", f"x_b{g}_lo", 4 * g)
                elif kind in ("lru_i0", "lru_i1"):
                    g = arg
                    for q in range(4):
                        dve.wait_ge(s(f"i{g}"), q + 1)
                        V.tensor_tensor(tc[:, q, :], tc[:, q, :], ta[:, q, :], MUL).then_inc(s(f"ix{g}"), 1)
                    more(j)
                    for q in range(4):
                        dve.wait_ge(s(f"t{g}"), q + 1)
                        dve.wait_ge(s(f"ix{g}"), q + 1)
                        link(V.tensor_scalar(ta[:, q, :], td[:, q, :], 1.0, None, ADD))
                        link(V.reciprocal(ta[:, q, :], ta[:, q, :]))
                        V.tensor_tensor(td[:, q, :], td[:, q, :], ta[:, q, :], MUL).then_inc(s(f"ratio{g}"), 1)
                        if q % 2 == 0:
                            more(j)
                    for q in range(4):
                        dve.wait_ge(s(f"a{g}"), q + 1)
                        dve.wait_ge(s(f"root_b{g}"), q + 1)
                        link(V.tensor_tensor(td[:, q, :], td[:, q, :], tc[:, q, :], MUL))
                        V.tensor_tensor_scan(tc[:, q, :], tb[:, q, :], td[:, q, :], 0.0, MUL, ADD).then_inc(s(f"y_b{g}_scan"), 1)
                elif kind in ("b_y0", "b_y1"):
                    g = arg // N - 5
                    for q in range(4):
                        dve.wait_ge(s(f"y_b{g}_scan"), q + 1)
                        dve.wait_ge(s(f"gelu{g}"), q + 1)
                        V.tensor_tensor(td[:, q, :], tc[:, q, :], ta[:, q, :], MUL).then_inc(s(f"y_b{g}_prod"), 1)
                    lo_of(td, f"y_b{g}_hi", f"y_b{g}_lo", 4 * g)
                elif kind == "w_o" and arg == 0:
                    wait_job(j)
                    dve.wait_ge(s("x_again"), 16)
                    for t in range(TT):
                        o = m_rows[:, t, 0:N]
                        V.tensor_tensor(o, o, ps[:, bank(j, t), :], ADD).then_inc(s("x_mid0"), 1)
                    dve.wait_ge(s("x_mid0"), 4)
                    dve.sem_inc(dve_read, 1)

            j = JOB["w_o1"]
            dve.wait_ge(s("norm_rows"), 32)
            for t in range(TT):
                dve.wait_ge(s("w_o_tile"), t + 1)
                o = m_rows[:, t, N:D]
                V.tensor_tensor(o, o, ps[:, bank(j, t), :], ADD).then_inc(s("x_mid"), 1)
                dve.wait_ge(s("sq2"), t + 1)
                V.tensor_scalar(stat[:, 1, t:t + 1], stat[:, 0, t:t + 1], 1.0 / D, EPS, MUL, ADD).then_inc(s("ms2"), 1)
                dve.wait_ge(s("root2"), t + 1)
                link(V.reciprocal(stat[:, 3, t:t + 1], stat[:, 2, t:t + 1]))
                if t >= 2:
                    dve.wait_ge(s(f"h2_out{t - 2}"), 16)
                    dve.wait_ge(s("h2_turned"), t - 1)
                V.scalar_tensor_tensor(out=h2_nat[t % 2], in0=m_rows[:, t, :], scalar=stat[:, 3, t:t + 1], in1=norm2_row,
                                       op0=MUL, op1=MUL).then_inc(s("h2"), 1)
            c0, i0 = MIX_CHUNKS, MIX_SUBS
            for k in range(2):
                moe_lo(i0, 0, c0, k)
            dve.wait_ge(s("router_in"), 64)
            lg, eg = logit[:, :, 0:NG], logit[:, :, NG:20]
            for t in range(TT):
                dve.wait_ge(s("logits"), t + 1)
                ins = V.tensor_tensor(logit[:, t, :], ps[:, bank(JOB["w_o1"], t), 0:20], b_r[:, :], ADD)
            link(ins)
            e_no, grp_of, g_no = rc[:, 0, :, :], rc[:, 1, :, :], rc[:, 2, :, 0:NG]

            def wide(v, n):
                return v.unsqueeze(2).to_broadcast([P, TT, n])

            link(V.tensor_reduce(r1[:, 0, :], lg, AX_X, ALU.max))
            link(V.tensor_tensor(rt[:, 6, :, 0:NG], lg, wide(r1[:, 0, :], NG), ALU.is_equal))
            link(V.tensor_tensor(rt[:, 6, :, 0:NG], rt[:, 6, :, 0:NG], g_no, MUL))
            link(V.tensor_reduce(r1[:, 1, :], rt[:, 6, :, 0:NG], AX_X, ALU.min))
            link(V.tensor_tensor(rt[:, 7, :, :], grp_of, wide(r1[:, 1, :], NE), ALU.is_equal))
            link(V.tensor_scalar(rt[:, 8, :, :], rt[:, 7, :, :], -1.0, BIG, ADD, MUL))
            link(V.tensor_tensor(rt[:, 8, :, :], rt[:, 8, :, :], eg, ADD))
            for k in range(2):
                if k:
                    link(V.scalar_tensor_tensor(out=rt[:, 8, :, :], in0=rt[:, 10, :, :], scalar=-3.0 * BIG, in1=rt[:, 8, :, :],
                                                op0=MUL, op1=ADD))
                link(V.tensor_reduce(r1[:, 2 + k, :], rt[:, 8, :, :], AX_X, ALU.max))
                link(V.tensor_tensor(rt[:, 9, :, :], rt[:, 8, :, :], wide(r1[:, 2 + k, :], NE), ALU.is_equal))
                link(V.tensor_tensor(rt[:, 9, :, :], rt[:, 9, :, :], e_no, MUL))
                link(V.tensor_reduce(r1[:, 4, :], rt[:, 9, :, :], AX_X, ALU.min))
                link(V.tensor_tensor(rt[:, 10 + k, :, :], e_no, wide(r1[:, 4, :], NE), ALU.is_equal))
            V.tensor_tensor(routed16[:, :, :], rt[:, 10, :, :], rt[:, 11, :, :], ADD).then_inc(s("routed"), 1)
            V.tensor_tensor(rt[:, 13, :, 0:NG], lg, wide(r1[:, 0, :], NG), SUB)
            V.tensor_tensor(r1[:, 5, :], r1[:, 3, :], r1[:, 2, :], SUB).then_inc(s("soft_in"), 1)
            dve.wait_ge(s("ranked"), 1)
            rb = bank(JOB["w_o0"], 0)
            link(V.tensor_copy(ranks, ps[:, rb, 0:(TT + 1) * NE]))
            rank, count = ranks[:, 0:TT * NE].rearrange("p (t e) -> p t e", e=NE), ranks[:, TT * NE:(TT + 1) * NE]
            link(V.scalar_tensor_tensor(out=r1[:, 11, :], in0=rank[:, :, 0], scalar=1.0, in1=routed16[:, :, 0], op0=ADD, op1=MUL))
            link(V.tensor_scalar(r1[:, 11, :], r1[:, 11, :], -1.0, None, ADD))
            V.tensor_tensor(slot_of[:, 0:TT, :], slot_iota[:, :].unsqueeze(1).to_broadcast([P, TT, P]), wide(r1[:, 11, :], P),
                            ALU.is_equal).then_inc(s("slots"), 1)
            link(V.tensor_scalar(cnt[:, 1, :], count, float(P), None, ALU.is_gt))
            dve.wait_ge(s("idx_sum"), 1)
            V.tensor_copy(idx[:, :], ps[:, 7, 0:1]).then_inc(s("idx_made"), 1)
            for k in range(2, 4):
                moe_lo(i0, 0, c0, k)
            for k in (2, 3):
                link(V.scalar_tensor_tensor(out=cnt[:, 1, :], in0=count, scalar=float(k * P), in1=cnt[:, 1, :],
                                            op0=ALU.is_gt, op1=ADD))
            V.memset(cnt[:, 3, :], 1.0)
            link(V.tensor_copy(cnt[:, 4, :], cnt[:, 1, :]))
            link(V.tensor_tensor_scan(cnt[:, 2, :], cnt[:, 3, :], cnt[:, 4, :], 0.0, MUL, ADD))
            link(V.tensor_tensor(cnt[:, 5, :], cnt[:, 2, :], cnt[:, 1, :], SUB))
            link(V.scalar_tensor_tensor(out=cnt[:, 5, :], in0=cnt[:, 5, :], scalar=float(P), in1=cnt[:, 0, :], op0=MUL, op1=ADD))
            link(V.tensor_scalar(rt[:, 12, :, :], rank, float(P), None, ALU.is_ge))
            link(V.tensor_tensor(rt[:, 12, :, :], rt[:, 12, :, :], cnt[:, 5, :].unsqueeze(1).to_broadcast([P, TT, NE]), MUL))
            link(V.tensor_tensor(rt[:, 12, :, :], rt[:, 12, :, :], rc[:, 3, :, :], ADD))
            link(V.tensor_tensor(rt[:, 12, :, :], rt[:, 12, :, :], rank, ADD))
            for k in range(2):
                link(V.tensor_tensor(rt[:, 9, :, :], rt[:, 12, :, :], rt[:, 10 + k, :, :], MUL))
                link(V.tensor_reduce(pos_rel[:, k, :], rt[:, 9, :, :], AX_X, ADD))

            def slots(b):
                dve.wait_ge(s("idx_sum"), b)
                V.tensor_scalar(pos_rel[:, :, :], pos_rel[:, :, :], -float(P), None, ADD).then_inc(s("pos_moved"), 1)
                dve.wait_ge(s("pos_moved"), b)
                V.tensor_tensor(slot_of, slot_iota[:, :].unsqueeze(1).to_broadcast([P, 2 * TT, P]),
                                pos_rel[:, :, :].rearrange("p k t -> p (k t)").unsqueeze(2).to_broadcast([P, 2 * TT, P]),
                                ALU.is_equal).then_inc(s("slots"), 1)

            def idx_of(b):
                dve.wait_ge(s("idx_sum"), b + 1)
                dve.wait_ge(s("sel_in"), 16 * b)
                V.tensor_copy(idx[:, :], ps[:, 7, 0:1]).then_inc(s("idx_made"), 1)

            def sel_lo(b):
                dve.wait_ge(s("sel_hi"), b + 1)
                V.tensor_tensor(h_lo[:, :, 0:P], ps[:, 4:6, :].rearrange("p a (k s) -> p (a k) s", s=P),
                                h_hi[:, :, 0:P], SUB).then_inc(s("sel_lo"), 1)

            def hid_of(b, first=False):
                dve.wait_ge(s("h3"), b + 1)
                dve.wait_ge(s("silu"), b + 1)
                if not first:
                    dve.wait_ge(s("hid_turned"), b)
                V.tensor_tensor(hid, ps[:, 1, :], silu, MUL).then_inc(s("hid"), 1)

            def hid_lo(b):
                dve.wait_ge(s("hid_hi"), b + 1)
                V.tensor_tensor(h_lo[:, 0:4, P:2 * P], ps[:, 6, :].rearrange("p (k s) -> p k s", s=P),
                                h_hi[:, 0:4, P:2 * P], SUB).then_inc(s("hid_lo"), 1)

            def y_half(b, first=False, last=False):
                dve.wait_ge(s("y"), b + 1)
                if not first and not last:
                    dve.wait_ge(s("y_stored"), 16 * b)
                V.tensor_copy((y_last if last else y_out)[:, N:D], ps[:, 3, :]).then_inc(s("y_dve"), 1)

            link(V.tensor_copy(pos_i[:, :, :], pos_rel[:, :, :]))
            slots(1)
            sel_lo(0)
            idx_of(1)
            link(V.tensor_tensor(xtra[:, :, :], cnt[0:1, 2, :].unsqueeze(1).to_broadcast([1, 8, NE]), xtra[:, :, :], ALU.is_le))
            link(V.tensor_reduce(xtra_n[:, :], xtra[:, :, :], AX_X, ADD))
            link(V.tensor_copy(xtra_i[:, 0:8], xtra_n[:, :]))
            V.tensor_copy(xtra_i[:, 8:9], cnt[0:1, 2, NE - 1:NE]).then_inc(s("extras_known"), 1)
            dve.wait_ge(s("soft_exp"), 2)
            link(V.tensor_reduce(r1[:, 7, :], rt[:, 14, :, 0:NG], AX_X, ADD))
            link(V.tensor_scalar(r1[:, 8, :], r1[:, 6, :], 1.0, None, ADD))
            link(V.tensor_tensor(r1[:, 8, :], r1[:, 8, :], r1[:, 7, :], MUL))
            link(V.reciprocal(r1[:, 9, :], r1[:, 8, :]))
            link(V.tensor_tensor(r1[:, 10, :], r1[:, 9, :], r1[:, 6, :], MUL))

            c1, i1 = MIX_CHUNKS + 4, MIX_SUBS + 8
            for k in range(4, 8):
                moe_lo(i0, 0, c0, k)
            slots(2)
            hid_of(0, first=True)
            sel_lo(1)
            for k in range(4):
                moe_lo(i1, 0, c1, k)
            idx_of(2)

            def body(e, ahead=True, turn_next=True, first=False):
                turn = e - 1
                for k in range(4, 8):
                    moe_lo(i1, turn, c1, k)
                hid_lo(e - 1)
                if ahead:
                    slots(e + 2)
                for k in range(8, 12):
                    moe_lo(i1, turn, c1, k)
                hid_of(e)
                if turn_next:
                    sel_lo(e + 1)
                for k in range(4):
                    moe_lo(i1, e, c1, k)
                if ahead:
                    idx_of(e + 2)
                y_half(e - 1, first)

            body(1, first=True)
            with dve.Fori(2, NE - 2) as e:
                body(e)
            body(NE - 2, ahead=False)
            body(NE - 1, ahead=False, turn_next=False)
            hid_lo(NE - 1)
            y_half(NE - 1, last=True)

            dve.wait_ge(s("extras_known"), 1)
            n_extra = dve.value_load(xtra_i[0:1, 8:9], min_val=0, max_val=EXTRAS)
            with dve.If(n_extra > 0):
                with dve.Fori(0, EXTRAS) as j:
                    with dve.If(n_extra > j):
                        b = NE + j
                        cx, ix = XTRA_BASE
                        slots(b)
                        idx_of(b)
                        sel_lo(b)
                        for k in range(8):
                            moe_lo(ix, j, cx, k)
                        hid_of(b)
                        for k in range(8, 12):
                            moe_lo(ix, j, cx, k)
                        hid_lo(b)
                        y_half(b)

            for t in range(TT):
                o = m_rows[:, t, :]
                for k in range(2):
                    dve.wait_ge(s(f"y_got{t}{k}"), 16)
                    ins = V.scalar_tensor_tensor(out=o, in0=y_got[t][k], scalar=r1[:, 9 + k, t:t + 1], in1=o, op0=MUL, op1=ADD)
                    if k == 0:
                        link(ins)
                    else:
                        ins.then_inc(s("merged"), 1)
                dve.wait_ge(s("sq3"), t + 1)
                V.tensor_scalar(stat[:, 5, t:t + 1], stat[:, 4, t:t + 1], 1.0 / D, EPS, MUL, ADD).then_inc(s("ms3"), 1)
                dve.wait_ge(s("root3"), t + 1)
                link(V.reciprocal(stat[:, 7, t:t + 1], stat[:, 6, t:t + 1]))
                V.scalar_tensor_tensor(out=y_got[t][0], in0=o, scalar=stat[:, 7, t:t + 1], in1=final_row,
                                       op0=MUL, op1=MUL).then_inc(s("final_rows"), 1)

        @block.tensor
        def _(pe):
            T = nc.tensor

            def three(o, a_hi, a_lo, b_hi, b_lo, start, stop):
                T.matmul(o, a_hi, b_hi, start=start, stop=False)
                T.matmul(o, a_hi, b_lo, start=False, stop=False)
                return T.matmul(o, a_lo, b_hi, start=False, stop=stop)

            pe.wait_ge(s("ident_made"), 1)
            pe.wait_ge(s("rows_in"), 8 * 16)
            T.transpose(ps[:, 7, 0:NROWS], rows[:, :], ident[0:NROWS, 0:NROWS]).then_inc(s("rows_turned"), 1)
            for t in range(TT):
                pe.wait_ge(s(f"x_scaled{t}"), 1)
                for k in range(KD):
                    if t == 0 and k == 7:
                        pe.wait_ge(s("cols_made"), 1)
                    ins = T.transpose(ps[:, k, t * P:(t + 1) * P], m_rows[:, t, k * P:(k + 1) * P], ident[:, :])
                    if t == TT - 1:
                        ins.then_inc(s("x_turned"), 1)

            def sub_ready(i):
                pe.wait_ge(lo_made, i + 1)

            def turn_h2(t):
                pe.wait_ge(s("h2"), t + 1)
                if t == 0:
                    pe.wait_ge(dve_read, dve_reads(JOB["w_o0"]))
                if t >= 2:
                    pe.wait_ge(s("h2_t"), t - 1)
                for k in range(KD):
                    ins = T.transpose(ps[:, bank(JOB["w_o0"], 2 * (t % 2) + k // 4), (k % 4) * P:(k % 4 + 1) * P],
                                      h2_nat[t % 2][:, k * P:(k + 1) * P], ident[:, :])
                ins.then_inc(s("h2_turned"), 1)

            def route(t):
                if t == 0:
                    pe.wait_ge(s("router_in"), 64)
                pe.wait_ge(s("h2_t"), t + 1)
                pe.wait_ge(s("x_mid"), t + 1)
                for k in range(KD):
                    ins = T.matmul(ps[:, bank(JOB["w_o1"], t), 0:20], h2_t[t % 2][:, k, :], w_r[:, k, :],
                                   start=(k == 0), stop=(k == KD - 1))
                ins.then_inc(s("logits"), 1)
            sub = [0]
            for j, (kind, arg, n) in enumerate(JOBS):
                if j < 2:
                    pe.wait_ge(s("h_lo"), 4 * j + 4)
                else:
                    if act_reads(j - 2):
                        pe.wait_ge(act_read, act_reads(j - 2))
                    if dve_reads(j - 2):
                        pe.wait_ge(dve_read, dve_reads(j - 2))
                if kind in ("lru_r0", "lru_i0", "lru_r1", "lru_i1", "pool"):
                    if kind == "pool":
                        pe.wait_ge(s("pooled_lo"), 4)
                        y0 = 4
                    else:
                        pe.wait_ge(s(f"x_b{arg}_lo"), 4)
                        y0 = 4 * arg
                    if kind[:5] != "lru_i":
                        sub_ready(sub[0])
                        sub[0] += 1
                    slot = (sub[0] - 1) % SUB_SLOTS
                    a = 1 if kind[:5] == "lru_i" else 0
                    for q in range(4):
                        c = slice(q * P, (q + 1) * P)
                        ins = three(ps[:, bank(j, q), :], w_hi[:, slot, a, c], w_lo[:, slot, a, c],
                                    y_hi[:, y0 + q, :], y_lo[:, y0 + q, :], True, True)
                    ins.then_inc(job_done, 1)
                    if kind[:5] != "lru_r":
                        pe.wait_ge(job_done, j + 1)
                        pe.sem_inc(sub_used, 1)
                    continue
                if kind == "w_o" and arg == 1:
                    for t in range(TT):
                        for i in range(4):
                            if t == 0:
                                sub_ready(sub[0] + i)
                            for k in range(2):
                                kk = 2 * i + k
                                c = slice(t * P, (t + 1) * P)
                                slot = (sub[0] + i) % SUB_SLOTS
                                ins = three(ps[:, bank(j, t), :], h_hi[:, kk, c], h_lo[:, kk, c],
                                            w_hi[:, slot, k, :], w_lo[:, slot, k, :], kk == 0, kk == KD - 1)
                            if t == TT - 1:
                                ins.then_inc(sub_used, 1)
                        if t < TT - 1:
                            ins.then_inc(s("w_o_tile"), 1)
                        if t == 1:
                            turn_h2(0)
                        elif t == 2:
                            route(0)
                            turn_h2(1)
                    pe.wait_ge(sub_used, sub[0] + 4)
                    pe.sem_inc(s("w_o_tile"), 1)
                    sub[0] += 4
                    route(1)
                    turn_h2(2)
                    route(2)
                    turn_h2(3)
                    route(3)
                    continue
                if kind == "a_out":
                    pe.wait_ge(s("y_a_lo"), 4)
                elif kind == "c_out":
                    pe.wait_ge(s("y_c_lo"), 4)
                elif kind == "b_out":
                    pe.wait_ge(s("y_b0_lo"), 4)
                rhs_hi, rhs_lo, y0 = (y_hi, y_lo, 4 if kind == "c_out" else 0) if "_out" in kind else (h_hi, h_lo, 0)
                for i in range(n):
                    sub_ready(sub[0])
                    if j == 0 and i > 1:
                        pe.wait_ge(s("h_lo"), 2 * i + 2)
                    if kind == "b_out" and i == 2:
                        pe.wait_ge(s("y_b1_lo"), 4)
                    if kind == "w_o":
                        pe.wait_ge(s("m_lo"), 2 * i + 2)
                    slot = sub[0] % SUB_SLOTS
                    for k in range(2):
                        kk = 2 * i + k
                        first, last = kk == 0, kk == 2 * n - 1
                        for q in range(4):
                            c = slice(q * P, (q + 1) * P)
                            if kind == "w_o":
                                ins = three(ps[:, bank(j, q), :], h_hi[:, kk, c], h_lo[:, kk, c],
                                            w_hi[:, slot, k, :], w_lo[:, slot, k, :], first, last)
                            else:
                                ins = three(ps[:, bank(j, q), :], w_hi[:, slot, k, c], w_lo[:, slot, k, c],
                                            rhs_hi[:, y0 + kk, :], rhs_lo[:, y0 + kk, :], first, last)
                    ins.then_inc(sub_used, 1)
                    sub[0] += 1
                pe.wait_ge(sub_used, sub[0])
                pe.sem_inc(job_done, 1)

            pe.wait_ge(s("routed"), 1)
            rb = bank(JOB["w_o0"], 0)
            for t in range(TT + 1):
                o = ps[:, rb, t * NE:(t + 1) * NE]
                for u in range(min(t + 1, TT)):
                    ins = T.matmul(o, ltri[:, :] if u == t else ones16[:, :], routed16[:, u, :],
                                   start=(u == 0), stop=(u == min(t, TT - 1)))
            ins.then_inc(s("ranked"), 1)

            def idx_sum(b, first=False):
                pe.wait_ge(s("slots"), b + 1)
                if not first:
                    pe.wait_ge(s("idx_made"), b)
                n = TT if first else 2 * TT
                for a in range(n):
                    ins = T.matmul(ps[:, 7, 0:1], slot_of[:, a, :], tok_id[:, a % TT:a % TT + 1],
                                   start=(a == 0), stop=(a == n - 1))
                ins.then_inc(s("idx_sum"), 1)

            def turn_sel(b, first=False):
                pe.wait_ge(s("sel_in"), 16 * (b + 1))
                if not first:
                    pe.wait_ge(s("sel_lo"), b)
                for k in range(KD):
                    ins = T.transpose(ps[:, 4 + k // 4, (k % 4) * P:(k % 4 + 1) * P], sel[:, k * P:(k + 1) * P], ident[:, :])
                ins.then_inc(s("sel_turned"), 1)

            def turn_hid(b, first=False):
                pe.wait_ge(s("hid"), b + 1)
                if not first:
                    pe.wait_ge(s("hid_lo"), b)
                for k in range(4):
                    ins = T.transpose(ps[:, 6, k * P:(k + 1) * P], hid[:, k * P:(k + 1) * P], ident[:, :])
                ins.then_inc(s("hid_turned"), 1)

            def up(b, i0, turn, k0, o, done):
                for i in range(4):
                    pe.wait_ge(lo_made, 12 * turn + (i0 + k0 + i + 1))
                    slot = (i0 + k0 + i) % SUB_SLOTS
                    for k in range(2):
                        kk = 2 * i + k
                        ins = three(o, h_hi[:, kk, 0:P], h_lo[:, kk, 0:P], w_hi[:, slot, k, :], w_lo[:, slot, k, :],
                                    kk == 0, kk == KD - 1)
                    ins.then_inc(sub_used, 1)
                pe.wait_ge(sub_used, 12 * turn + (i0 + k0 + 4))
                pe.sem_inc(s(done), 1)

            def down(b, i0, turn, k0):
                for i in range(4):
                    pe.wait_ge(lo_made, 12 * turn + (i0 + k0 + i + 1))
                    slot = (i0 + k0 + i) % SUB_SLOTS
                    for k in range(2):
                        kk = 2 * (i % 2) + k
                        ins = three(ps[:, 2 + i // 2, :], h_hi[:, kk, P:2 * P], h_lo[:, kk, P:2 * P],
                                    w_hi[:, slot, k, :], w_lo[:, slot, k, :], kk == 0, kk == 3)
                    ins.then_inc(sub_used, 1)
                pe.wait_ge(sub_used, 12 * turn + (i0 + k0 + 4))
                pe.sem_inc(s("y"), 1)

            def w1_of(b, i0, turn, first=False):
                pe.wait_ge(s("sel_lo"), b + 1)
                if not first:
                    pe.wait_ge(s("silu"), b)
                up(b, i0, turn, 0, ps[:, 0, :], "h1")

            def w3_of(b, i0, turn, first=False):
                if not first:
                    pe.wait_ge(s("hid"), b)
                up(b, i0, turn, 4, ps[:, 1, :], "h3")

            def w2_of(b, i0, turn, k0, first=False):
                pe.wait_ge(s("hid_lo"), b + 1)
                if not first:
                    pe.wait_ge(s("y_act"), b)
                    pe.wait_ge(s("y_dve"), b)
                down(b, i0, turn, k0)

            i0, i1 = MIX_SUBS, MIX_SUBS + 8
            idx_sum(0, first=True)
            turn_sel(0, first=True)
            idx_sum(1)
            w1_of(0, i0, 0, first=True)
            w3_of(0, i0, 0, first=True)
            turn_sel(1)
            idx_sum(2)

            def body(e, first=False, ahead=True, turn_next=True):
                w1_of(e, i1, e - 1)
                turn_hid(e - 1, first)
                w3_of(e, i1, e - 1)
                if turn_next:
                    turn_sel(e + 1)
                if ahead:
                    idx_sum(e + 2)
                w2_of(e - 1, i1, e - 1, 8, first)

            body(1, first=True)
            with pe.Fori(2, NE - 2) as e:
                body(e)
            body(NE - 2, ahead=False)
            body(NE - 1, ahead=False, turn_next=False)
            turn_hid(NE - 1)
            w2_of(NE - 1, i1, NE - 1, 0)

            pe.wait_ge(s("extras_known"), 1)
            n_extra = pe.value_load(xtra_i[0:1, 8:9], min_val=0, max_val=EXTRAS)
            with pe.If(n_extra > 0):
                with pe.Fori(0, EXTRAS) as j:
                    with pe.If(n_extra > j):
                        b = NE + j
                        ix = XTRA_BASE[1]
                        idx_sum(b)
                        turn_sel(b)
                        w1_of(b, ix, j)
                        w3_of(b, ix, j)
                        turn_hid(b)
                        w2_of(b, ix, j, 8)


_INS = ["x", "norm1_g", "w_in", "conv_a_w", "w_a_out", "conv_b_w", "conv_b_b", "lru_wa", "lru_ba", "lru_wx",
        "lru_bx", "lru_lambda", "w_b_out", "pool_w", "pool_scale", "w_c_out", "w_o", "norm2_g", "router_grp_w",
        "router_grp_b", "router_exp_w", "router_exp_b", "moe_w1", "moe_w3", "moe_w2", "final_g"]


def kernel(**inputs):
    import numpy as _np
    import concourse.bacc as _bacc
    from concourse import mybir as _mybir
    from concourse.bass_utils import run_bass_kernel_spmd as _run

    nc = _bacc.Bacc("TRN2", target_bir_lowering=False, num_devices=1)
    arrays, args = {}, []
    for name in _INS:
        a = _np.ascontiguousarray(inputs[name])
        arrays[f"in_{name}_dram"] = a
        args.append(nc.dram_tensor(f"in_{name}_dram", a.shape, _mybir.dt.from_np(a.dtype), kind="ExternalInput").ap())
    args.append(nc.dram_tensor("out_0_dram", (1, SEQ, D), F32, kind="ExternalOutput").ap())
    trunk(nc, *args)
    r = _run(nc, [arrays], core_ids=[0])
    return r.results[0]["out_0_dram"]
```

```python
from contextlib import ExitStack

import concourse.bass as bass
from concourse import mybir

P = 128
SEQ, D = 512, 1024
TT = SEQ // P
KD = D // P
NE, NG, EPG = 16, 4, 4
DE = 512
N = 512
RAW_SLOTS = 6
SUB_SLOTS = 4
EXTRAS = 7
SLOTS = (NE + EXTRAS) * P
WINDOWS = (2, 4, 8, 16)
BIG = 1.0e30
EPS = 1e-6

F32, F32R = mybir.dt.float32, mybir.dt.float32r
F16, I32, U32 = mybir.dt.float16, mybir.dt.int32, mybir.dt.uint32
ALU = mybir.AluOpType
ACT = mybir.ActivationFunctionType
AX_X = mybir.AxisListType.X
MUL, ADD, SUB = ALU.mult, ALU.add, ALU.subtract

JOBS = [
    ("a_c", 512, 4), ("a_x", 1024, 4), ("a_b", 0, 4), ("c_u", 3584, 4),
    ("gate", 4096, 4), ("pool", 0, 1), ("a_out", 0, 2), ("gate", 4608, 4), ("a_out", 1, 2),
    ("b_x0", 1536, 4), ("gate", 6144, 4), ("c_out", 0, 2), ("lru_r0", 0, 1), ("lru_i0", 0, 0),
    ("gate", 6656, 4), ("c_out", 1, 2), ("b_y0", 2560, 4),
    ("b_x1", 2048, 4), ("gate", 5120, 4), ("lru_r1", 1, 1), ("lru_i1", 1, 0), ("b_y1", 3072, 4),
    ("gate", 5632, 4), ("b_out", 0, 4), ("b_out", 1, 4), ("w_o", 0, 4), ("w_o", 1, 4),
]
NJ = len(JOBS)
TITLES = []
for _kind, _arg, _n in JOBS:
    _same = sum(t.rstrip("0123456789") == _kind for t in TITLES)
    TITLES.append(_kind if _kind[-1] in "01" or _kind in ("a_c", "a_x", "a_b", "c_u", "pool") else f"{_kind}{_same}")
JOB = {t: i for i, t in enumerate(TITLES)}

SUBS, CHUNK_OF_JOB = [], []
_c = 0
for _j, (_kind, _arg, _n) in enumerate(JOBS):
    CHUNK_OF_JOB.append(_c)
    for _i in range(_n):
        SUBS.append((_j, _c + _i // 2, _i % 2, _i))
    _c += (_n + 1) // 2
MIX_CHUNKS, MIX_SUBS = _c, len(SUBS)
SUBS_BEFORE = [sum(1 for s in SUBS if s[0] < j) for j in range(NJ + 1)]
assert MIX_SUBS == SUBS_BEFORE[NJ]

ROWS = {}
_r = 0
for _name, _n in (("norm1_g", 8), ("conv_a_w", 12), ("conv_b_w", 32), ("conv_b_b", 8),
                  ("lru_ba", 8), ("lru_bx", 8), ("lru_lambda", 8), ("pool_scale", 4)):
    ROWS[_name] = _r
    _r += _n
NROWS = _r


def trunk(nc, x, norm1_g, w_in, conv_a_w, w_a_out, conv_b_w, conv_b_b, lru_wa, lru_ba, lru_wx,
          lru_bx, lru_lambda, w_b_out, pool_w, pool_scale, w_c_out, w_o, norm2_g, router_grp_w,
          router_grp_b, router_exp_w, router_exp_b, moe_w1, moe_w3, moe_w2, final_g, out):
    x_rows = x.rearrange("b (t p) d -> (b t) p d", p=P)
    out_rows = out.rearrange("b (t p) d -> (b t) p d", p=P)

    def chunks_of(w):
        return w.rearrange("(c k p) (m n) -> c m p k n", p=P, k=4, n=N)

    w_in_c, w_a_c, w_b_c, w_c_c, w_o_c = (chunks_of(w[0]) for w in (w_in, w_a_out, w_b_out, w_c_out, w_o))
    w1_c = moe_w1.rearrange("l e (c k p) n -> (l e) c p k n", p=P, k=4)
    w3_c = moe_w3.rearrange("l e (c k p) n -> (l e) c p k n", p=P, k=4)
    w2_c = moe_w2.rearrange("l e (k p) (c n) -> (l e) c p k n", p=P, n=N)

    y_dram = nc.dram_tensor("expert_rows", (SLOTS, D), F32, kind="Internal").ap()
    y_blocks = y_dram.rearrange("(b p) d -> b p d", p=P)

    with ExitStack() as ctx:
        def sb(name, shape, dt=F32):
            return ctx.enter_context(nc.sbuf_tensor(name, shape, dt))

        def sem(name):
            return ctx.enter_context(nc.semaphore(name))

        ps = ctx.enter_context(nc.psum_tensor("ps", [P, 8, N], F32))

        raw = sb("raw", [P, RAW_SLOTS, 4, N])
        w_hi = sb("w_hi", [P, SUB_SLOTS, 2, N], F32R)
        w_lo = sb("w_lo", [P, SUB_SLOTS, 2, N], F32R)
        h_hi = sb("h_hi", [P, KD, SEQ], F32R)
        h_lo = sb("h_lo", [P, KD, SEQ], F32R)
        y_hi = sb("y_hi", [P, KD, SEQ], F32R)
        y_lo = sb("y_lo", [P, KD, SEQ], F32R)
        m = sb("m", [P, 4 * D])
        sg = sb("sg", [P, 4, SEQ])
        ta = sb("ta", [P, 4, SEQ])
        tb = sb("tb", [P, 4, SEQ])
        tc = sb("tc", [P, 4, SEQ])
        td = sb("td", [P, 4, SEQ])
        ident = sb("ident", [P, P])
        rows = sb("rows", [NROWS, P])
        cols = sb("cols", [P, NROWS])
        c8 = sb("c8", [P, 10, KD])
        inv_cnt = sb("inv_cnt", [P, 4, 16])
        stat = sb("stat", [P, 8, TT])
        ltri = sb("ltri", [P, P], F16)
        ones16 = sb("ones16", [P, P], F16)
        slot_iota = sb("slot_iota", [P, P])
        w_r = sb("w_r", [P, KD, 20])
        b_r = sb("b_r", [P, 20])
        rc = sb("rc", [P, 4, TT, NE])
        r1 = sb("r1", [P, 12, TT])
        routed16 = sb("routed16", [P, TT, NE], F16)
        cnt = sb("cnt", [P, 6, NE])
        pos_i = sb("pos_i", [P, 2, TT], I32)
        pos_rel = sb("pos_rel", [P, 2, TT])
        pos_two = sb("pos_two", [P, 2, TT])
        tick = sb("tick", [P, 1], F16)
        xtra_at = sb("xtra_at", [P, EXTRAS + 2, TT])
        eps_col = sb("eps_col", [P, 1])
        xtra = sb("xtra", [1, 8, NE])
        xtra_n = sb("xtra_n", [1, 8])
        xtra_i = sb("xtra_i", [1, 9], I32)

        m_rows = m[:, :].rearrange("p (t d) -> p t d", d=D)
        mt = m[:, :].rearrange("p (k s) -> p k s", s=SEQ)
        flat = {n: t[:, :, :].rearrange("p a b -> p (a b)") for n, t in (("ta", ta), ("tb", tb), ("tc", tc), ("td", td))}
        norm2_row, final_row = flat["tb"][:, 0:D], flat["tb"][:, D:2 * D]
        h2_nat = [flat["td"][:, 0:D], flat["td"][:, D:2 * D]]
        h2_t = [flat["tc"][:, i * D:(i + 1) * D].rearrange("p (k s) -> p k s", s=P) for i in range(2)]
        hid = flat["ta"][:, D:D + DE]
        silu = flat["ta"][:, D + DE:D + 2 * DE]
        y_out = flat["tc"][:, 0:D]
        y_last = flat["td"][:, 0:D]
        y_got = [[raw[:, t, 2 * k:2 * k + 2, :].rearrange("p a b -> p (a b)") for k in range(2)] for t in range(TT)]
        rt = sg[:, 1:3, :].rearrange("p a (b t e) -> p (a b) t e", t=TT, e=NE)
        logit = sg[:, 3, 0:20 * TT].rearrange("p (t e) -> p t e", e=20)
        slot_tab = sg[:, 0, 0:(NE + EXTRAS + 2) * TT].rearrange("p (b t) -> p b t", t=TT)
        one_hot = h_hi[:, 4:4 + TT, 2 * P:4 * P]
        hid_t_hi, hid_t_lo = h_hi[:, 0:4, 2 * P:3 * P], h_lo[:, 0:4, 2 * P:3 * P]
        ranks = sg[:, 3, P:P + (TT + 1) * NE]
        rows_hi = y_hi[:, :, :].rearrange("p (t a) s -> p t (a s)", t=TT)
        rows_lo = y_lo[:, :, :].rearrange("p (t a) s -> p t (a s)", t=TT)

        raw_in = [sem(f"raw_in{i}") for i in range(RAW_SLOTS)]
        hi_made, lo_made, sub_used = sem("hi_made"), sem("lo_made"), sem("sub_used")
        act_read, dve_read = sem("act_read"), sem("dve_read")
        named = {}

        def s(name):
            if name not in named:
                named[name] = sem(name)
            return named[name]

        reader = {"a_c": "act", "a_x": "dve", "a_b": "dve", "c_u": "act", "gate": "act", "pool": "both",
                  "a_out": "dve", "c_out": "dve", "b_out": "dve", "lru_r0": "act", "lru_i0": "act",
                  "lru_r1": "act", "lru_i1": "act", "b_x0": "both", "b_x1": "both", "b_y0": "act",
                  "b_y1": "act", "w_o": "dve"}

        def act_reads(j):
            return sum(reader[k] in ("act", "both") for k, _, _ in JOBS[:j + 1])

        def dve_reads(j):
            return sum(reader[k] in ("dve", "both") for k, _, _ in JOBS[:j + 1])

        def subs_by(j):
            through = SUBS_BEFORE[j] if JOBS[j][0][:5] == "lru_r" else SUBS_BEFORE[j + 1]
            return min(MIX_SUBS, through + SUB_SLOTS - (JOBS[min(j + 1, NJ - 1)][2] < 4))

        def most_by(j):
            return min(MIX_SUBS, max(SUBS_BEFORE[min(j + 3, NJ)], SUBS_BEFORE[min(j + 2, NJ)] + SUB_SLOTS))

        def wait_job(engine, j):
            kind, arg, _ = JOBS[j]
            if kind[:5] == "lru_r":
                engine.wait_ge(s("lru_r_done"), arg + 1)
            else:
                engine.wait_ge(sub_used, SUBS_BEFORE[j + 1])

        def half_bank(h):
            return ps[:, 4 + 2 * h:6 + 2 * h, :].rearrange("p a (k s) -> p (a k) s", s=2 * P)

        def half_of(tokens, h):
            return tokens[:, 4 * h:4 * h + 4, 0:2 * P]

        def gate_of(g):
            return tb if g == 5 else sg

        def bank(j, q):
            return 4 * (j % 2) + q

        def col(name, i):
            r = ROWS[name] + i
            return cols[:, r:r + 1]

        def mix_sub(i):
            j, c, half, _ = SUBS[i]
            t = raw[:, c % RAW_SLOTS, 2 * half:2 * half + 2, :]
            if JOBS[j][0] == "pool":
                return raw[:, c % RAW_SLOTS, 0:1, :], 1
            return t, 2

        ROW_PARAMS = (("conv_b_w", conv_b_w, 32), ("norm1_g", norm1_g, 8), ("conv_a_w", conv_a_w, 12),
                      ("pool_scale", pool_scale, 4), ("conv_b_b", conv_b_b, 8), ("lru_ba", lru_ba, 8),
                      ("lru_bx", lru_bx, 8), ("lru_lambda", lru_lambda, 8))

        def load_rows(engine, params, arrived):
            for name, w, k in params:
                src = w if len(w.shape) == 2 else w.rearrange("l a c -> l (a c)")
                engine.dma_start(rows[ROWS[name]:ROWS[name] + k, :],
                                 src.rearrange("l (r c) -> (l r) c", c=P)).then_inc(s(arrived), 16)

        block = ctx.enter_context(nc.Block())

        def body_base(e):
            return (MIX_CHUNKS, MIX_SUBS, 0) if isinstance(e, int) and e == 0 else (MIX_CHUNKS + 4, MIX_SUBS + 8, e - 1)

        XTRA_BASE = (MIX_CHUNKS + 6 * NE, MIX_SUBS + 12 * NE)

        @block.sync
        def _(sp):
            def load(c0, turn, dst, src, subs_before):
                slot = c0 % RAW_SLOTS
                if subs_before is not None:
                    sp.wait_ge(lo_made, subs_before)
                sp.dma_start(dst, src).then_inc(raw_in[slot], 16)

            def chunk_end(c):
                if c < MIX_CHUNKS:
                    return sum(1 for q in SUBS if q[1] <= c)
                return MIX_SUBS + 2 * (c - MIX_CHUNKS + 1)

            for t in range(TT):
                sp.dma_start(m_rows[:, t, :], x_rows[t]).then_inc(s(f"x_in{t}"), 16)
            for j, (kind, arg, n) in enumerate(JOBS):
                for i in range((n + 1) // 2):
                    c = CHUNK_OF_JOB[j] + i
                    slot = c % RAW_SLOTS
                    free = chunk_end(c - RAW_SLOTS) if c >= RAW_SLOTS else None
                    if c == 1:
                        sp.wait_ge(s("rows_in"), 4 * 16)
                        sp.wait_ge(s("more_rows_in"), 4 * 16)
                    dst = raw[:, slot, :, :]
                    if kind in ("lru_r0", "lru_r1"):
                        h = slice(4 * arg, 4 * arg + 4)
                        if free is not None:
                            sp.wait_ge(lo_made, free)
                        for a, w in enumerate((lru_wa, lru_wx)):
                            sp.dma_start(raw[:, slot, a, :].rearrange("p (h j) -> p h j", j=P),
                                         w[0, h].rearrange("h i j -> i h j")).then_inc(s(f"lru_in{arg}"), 16)
                        sp.sem_inc(raw_in[slot], 16)
                        continue
                    if kind == "pool":
                        if free is not None:
                            sp.wait_ge(lo_made, free)
                        sp.dma_start(raw[:, slot, 0, :].rearrange("p (h j) -> p h j", j=P),
                                     pool_w[0].rearrange("h i j -> i h j")).then_inc(raw_in[slot], 16)
                        continue
                    if kind in ("a_out", "b_out", "c_out"):
                        src = {"a_out": w_a_c, "b_out": w_b_c, "c_out": w_c_c}[kind][i, arg]
                    elif kind == "w_o":
                        src = w_o_c[i, arg]
                    else:
                        src = w_in_c[i, arg // N]
                    load(c, 0, dst, src, free)

            def expert_chunk(c0, turn, src):
                load(c0, turn, raw[:, c0 % RAW_SLOTS, :, :], src,
                     12 * turn + chunk_end(c0 - RAW_SLOTS))

            for i, w in enumerate((w1_c, w1_c, w3_c, w3_c)):
                expert_chunk(MIX_CHUNKS + i, 0, w[0, i % 2])

            def body(e, last=False):
                c0 = MIX_CHUNKS + 4
                turn = e - 1
                if not last:
                    for i, w in enumerate((w1_c, w1_c, w3_c, w3_c)):
                        expert_chunk(c0 + i, turn, w[e, i % 2])
                for i in range(2):
                    expert_chunk(c0 + (i if last else 4 + i), turn, w2_c[e - 1, i])

            with sp.Fori(1, NE) as e:
                body(e)
            body(NE, last=True)

            sp.wait_ge(s("y_last"), 2)
            sp.dma_start(y_blocks[NE - 1], y_last).then_inc(s("y_last_stored"), 16)

            sp.wait_ge(s("extras_known"), 1)
            n_extra = sp.value_load(xtra_i[0:1, 8:9], min_val=0, max_val=EXTRAS)
            with sp.If(n_extra > 0):
                with sp.Fori(0, EXTRAS) as j:
                    with sp.If(n_extra > j):
                        e = sp.value_load(xtra_i[0:1, bass.ds(j, 1)], min_val=0, max_val=NE - 1)
                        c0 = XTRA_BASE[0]
                        for i, w in enumerate((w1_c, w1_c, w3_c, w3_c, w2_c, w2_c)):
                            expert_chunk(c0 + i, j, w[e, i % 2])

            for t in range(TT):
                sp.wait_ge(s("final_rows"), t + 1)
                sp.dma_start(out_rows[t], y_got[t][0]).then_inc(s(f"stored{t}"), 16)
            for t in range(TT):
                sp.wait_ge(s(f"stored{t}"), 16)

        @block.gpsimd
        def _(pool):
            nc.gpsimd.memset(eps_col[:, :], EPS).then_inc(s("eps_made"), 1)
            nc.gpsimd.memset(ident[:, :], 0.0).then_inc(s("pool_step"), 1)
            pool.wait_ge(s("pool_step"), 1)
            nc.gpsimd.affine_select(out=ident[:, :], in_=ident[:, :], compare_op=ALU.not_equal, fill=1.0, base=0,
                                    pattern=[[-1, P]], channel_multiplier=1).then_inc(s("ident_made"), 1)
            load_rows(pool, ROW_PARAMS[4:], "more_rows_in")
            pool.dma_start(w_r[:, :, 0:NG], router_grp_w[0].rearrange("(k p) g -> p k g", p=P)).then_inc(s("router_in"), 16)
            pool.dma_start(w_r[:, :, NG:20], router_exp_w[0].rearrange("(k p) g -> p k g", p=P)).then_inc(s("router_in"), 16)
            pool.dma_start(b_r[:, 0:NG], router_grp_b.partition_broadcast(P)).then_inc(s("router_in"), 16)
            pool.dma_start(b_r[:, NG:20], router_exp_b.partition_broadcast(P)).then_inc(s("router_in"), 16)
            nc.gpsimd.iota(slot_iota[:, :], pattern=[[1, P]], base=0, channel_multiplier=0,
                           allow_small_or_imprecise_dtypes=True).then_inc(s("iotas"), 1)
            nc.gpsimd.iota(xtra_at[:, :, :], pattern=[[-P, EXTRAS + 2], [0, TT]], base=-NE * P, channel_multiplier=0,
                           allow_small_or_imprecise_dtypes=True).then_inc(s("iotas"), 1)
            nc.gpsimd.iota(rc[:, 0, :, :], pattern=[[0, TT], [1, NE]], base=-32, channel_multiplier=0,
                           allow_small_or_imprecise_dtypes=True).then_inc(s("iotas"), 1)
            nc.gpsimd.iota(rc[:, 1, :, :].rearrange("p t (g e) -> p t g e", e=EPG), pattern=[[0, TT], [1, NG], [0, EPG]],
                           base=-8, channel_multiplier=0, allow_small_or_imprecise_dtypes=True).then_inc(s("iotas"), 1)
            nc.gpsimd.iota(rc[:, 2, :, 0:NG], pattern=[[0, TT], [1, NG]], base=-8, channel_multiplier=0,
                           allow_small_or_imprecise_dtypes=True).then_inc(s("iotas"), 1)
            nc.gpsimd.iota(rc[:, 3, :, :], pattern=[[0, TT], [P, NE]], base=0, channel_multiplier=0,
                           allow_small_or_imprecise_dtypes=True).then_inc(s("iotas"), 1)
            nc.gpsimd.iota(cnt[:, 0, :], pattern=[[-P, NE]], base=(NE - 1) * P, channel_multiplier=0,
                           allow_small_or_imprecise_dtypes=True).then_inc(s("iotas"), 1)
            nc.gpsimd.iota(xtra[:, :, :], pattern=[[1, 8], [0, NE]], base=0, channel_multiplier=0,
                           allow_small_or_imprecise_dtypes=True).then_inc(s("iotas"), 1)
            nc.gpsimd.iota(inv_cnt[:, :, :], pattern=[[0, 4], [1, 16]], base=1, channel_multiplier=0,
                           allow_small_or_imprecise_dtypes=True).then_inc(s("iotas"), 1)
            nc.gpsimd.memset(ones16[:, :], 1.0).then_inc(s("pool_step"), 1)
            pool.wait_ge(s("pool_step"), 2)
            nc.gpsimd.affine_select(out=ltri[:, :], in_=ones16[:, :], compare_op=ALU.is_gt, fill=0.0, base=0,
                                    pattern=[[1, P]], channel_multiplier=-1).then_inc(s("iotas"), 1)

            flat_x = x.rearrange("b t d -> (b t) d")
            pool.wait_ge(s("y_a"), 4)
            for at in range(NE * P, SLOTS, SEQ):
                n_rows = min(SEQ, SLOTS - at)
                pool.dma_start(y_dram[at:at + n_rows, :], flat_x[0:n_rows, :]).then_inc(s(f"filled{at}"), 16)
            for at in range(NE * P, SLOTS, SEQ):
                pool.wait_ge(s(f"filled{at}"), 16)

            pool.wait_ge(s("gated"), 24)
            pool.dma_start(norm2_row, norm2_g.partition_broadcast(P)).then_inc(s("norm_rows"), 16)
            pool.dma_start(final_row, final_g.rearrange("(l d) -> l d", l=1).partition_broadcast(P)).then_inc(s("norm_rows"), 16)
            pool.wait_ge(s("m_split"), 2)
            pool.dma_start(m_rows, x_rows.rearrange("t p d -> p t d")).then_inc(s("x_again"), 16)

            def carry_waits(n):
                if not (isinstance(n, int) and n == 0):
                    pool.wait_ge(s("ticks"), n)
                nc.gpsimd.tensor_tensor(tick[:, :], ones16[:, 0:1], ones16[:, 0:1], MUL).then_inc(s("ticks"), 1)

            def store(b, n):
                pool.wait_ge(s("y_left"), n + 1)
                pool.wait_ge(s("y_right"), n + 1)
                carry_waits(n)
                pool.dma_start(y_blocks[b], y_out).then_inc(s("y_stored"), 16)

            store(0, 0)
            with pool.Fori(1, NE - 1) as e:
                store(e, e)

            def fetch(k, source):
                for t in range(TT):
                    nc.gpsimd.indirect_dma_start(out=y_got[t][k], out_offset=None, in_=source,
                                                 in_offset=bass.IndirectOffsetOnAxis(ap=pos_i[:, k, t:t + 1], axis=0)
                                                 ).then_inc(s(f"y_got{t}{k}"), 16)

            pool.wait_ge(s("extras_known"), 1)
            n_extra = pool.value_load(xtra_i[0:1, 8:9], min_val=0, max_val=EXTRAS)
            with pool.If(n_extra < 1):
                pool.wait_ge(lo_made, MIX_SUBS + 12 * NE)
                pool.wait_ge(s("y_stored"), 16 * (NE - 1))
                fetch(0, y_dram[0:(NE - 1) * P, :])
            pool.wait_ge(s("y_last_stored"), 16)
            with pool.If(n_extra > 0):
                with pool.Fori(0, EXTRAS) as j:
                    with pool.If(n_extra > j):
                        store(NE + j, NE - 1 + j)
                        pool.wait_ge(s("y_stored"), 16 * (NE + j))
                fetch(0, y_dram[:, :])
            fetch(1, y_dram[:, :])

        @block.scalar
        def _(act):
            made = [0]

            def hi_sub(dst_slot, src, cols_n):
                nc.scalar.activation(w_hi[:, dst_slot, 0:cols_n, :], src, ACT.Copy).then_inc(hi_made, 1)

            def split_next():
                i = made[0]
                j, c, half, _ = SUBS[i]
                if JOBS[j][0].startswith("lru"):
                    act.wait_ge(s(f"lru_in{JOBS[j][1]}"), 32)
                act.wait_ge(raw_in[c % RAW_SLOTS], 16 * (c // RAW_SLOTS + 1))
                if i >= SUB_SLOTS:
                    act.wait_ge(sub_used, i - SUB_SLOTS + 1)
                t, n = mix_sub(i)
                hi_sub(i % SUB_SLOTS, t, n)
                made[0] += 1

            def split_for(j):
                while made[0] < subs_by(j):
                    split_next()

            def more(j):
                if made[0] < most_by(j):
                    split_next()

            def moe_hi(i0, turn, c0, k):
                c = c0 + k // 2
                act.wait_ge(raw_in[c % RAW_SLOTS], 16 * (turn + c // RAW_SLOTS + 1))
                act.wait_ge(sub_used, 12 * turn + (i0 + k - SUB_SLOTS + 1))
                hi_sub((i0 + k) % SUB_SLOTS, raw[:, c % RAW_SLOTS, 2 * (k % 2):2 * (k % 2) + 2, :], 2)

            act.wait_ge(s("eps_made"), 1)
            nc.scalar.activation(stat[:, 5, 0:1], eps_col[:, :], ACT.Sqrt).then_inc(s("table_in"), 1)
            load_rows(act, ROW_PARAMS[:4], "rows_in")
            for t in range(TT):
                if t % 2 == 0:
                    act.wait_ge(s(f"x_in{t}"), 16)
                    nc.scalar.activation(flat["ta"][:, t // 2 * D:(t // 2 + 1) * D], m_rows[:, t, :],
                                         ACT.Square, accum_out=stat[:, 0, t:t + 1]).then_inc(s(f"sq1_{t}"), 1)
                act.wait_ge(s(f"sq1_{t}"), 1)
                nc.scalar.activation(stat[:, 2, t:t + 1], stat[:, 0, t:t + 1], ACT.Sqrt, scale=1.0 / D,
                                     bias=eps_col[:, :]).then_inc(s("root1"), 1)
            split_next()
            split_next()
            act.wait_ge(s("cols_made"), 1)
            for k in range(KD):
                if k == 4 or k == 6:
                    split_next()
                act.wait_ge(s("x_turned"), k + 1)
                nc.scalar.activation(h_hi[:, k, :], ps[:, k, :], ACT.Identity, scale=col("norm1_g", k)).then_inc(s("h_hi"), 1)
            lam = cols[:, ROWS["lru_lambda"]:ROWS["lru_lambda"] + KD]
            nc.scalar.activation(c8[:, 0, :], lam, ACT.Abs).then_inc(s("abs_lam"), 1)
            act.wait_ge(s("abs_lam"), 1)
            nc.scalar.activation(c8[:, 1, :], c8[:, 0, :], ACT.Exp, scale=-1.0).then_inc(s("exp_lam"), 1)

            def hi_of(src, name_in, name_out, y0, src_wait=None):
                for q in range(4):
                    act.wait_ge(s(name_in), q + 1)
                    nc.scalar.activation(y_hi[:, y0 + q, :], src[:, q, :], ACT.Copy).then_inc(s(name_out), 1)

            for j, (kind, arg, n) in enumerate(JOBS):
                title = TITLES[j]
                split_for(j)
                if kind == "a_c":
                    wait_job(act, j)
                    for q in range(4):
                        ins = nc.scalar.activation(tb[:, q, :], ps[:, bank(j, q), :], ACT.Copy).then_inc(s("a_c"), 1)
                    act.wait_ge(s("a_c"), 4)
                    act.sem_inc(act_read, 1)
                elif kind == "a_b":
                    hi_of(ta, "y_a", "y_a_hi", 0)
                elif kind == "c_u":
                    wait_job(act, j)
                    act.wait_ge(s("a_u"), 4)
                    for q in range(4):
                        nc.scalar.activation(tb[:, q, :], ps[:, bank(j, q), :], ACT.Copy).then_inc(s("c_u"), 1)
                    act.wait_ge(s("c_u"), 4)
                    act.sem_inc(act_read, 1)
                    hi_of(td, "pooled", "pooled_hi", 4)
                elif kind == "gate":
                    g = int(title[4:])
                    wait_job(act, j)
                    if g == 5:
                        act.wait_ge(s("y_b1_scan"), 4)
                    elif g:
                        act.wait_ge(s("gated"), 4 * g)
                    for q in range(4):
                        nc.scalar.activation(gate_of(g)[:, q, :], ps[:, bank(j, q), :], ACT.Sigmoid).then_inc(s("gate"), 1)
                    act.wait_ge(s("gate"), 4 * g + 4)
                    act.sem_inc(act_read, 1)
                elif kind == "pool":
                    wait_job(act, j)
                    for q in range(4):
                        nc.scalar.activation(y_hi[:, 4 + q, :], ps[:, bank(j, q), :], ACT.Identity,
                                             scale=col("pool_scale", q)).then_inc(s("y_c_hi"), 1)
                    act.wait_ge(s("y_c_hi"), 4)
                    act.sem_inc(act_read, 1)
                elif kind in ("b_x0", "b_x1"):
                    g = arg // N - 3
                    wait_job(act, j)
                    if g == 0:
                        act.wait_ge(s("y_a_lo"), 4)
                    else:
                        act.wait_ge(s("y_b0_prod"), 4)
                    for q in range(4):
                        c = 4 * g + q
                        nc.scalar.activation(ta[:, q, :], ps[:, bank(j, q), :], ACT.Identity,
                                             scale=col("conv_b_w", 3 * KD + c), bias=col("conv_b_b", c)).then_inc(s(f"x_b{g}_tap"), 1)
                    act.wait_ge(s(f"x_b{g}_tap"), 4)
                    act.sem_inc(act_read, 1)
                    hi_of(ta, f"x_b{g}", f"x_b{g}_hi", 4 * g)
                elif kind in ("lru_r0", "lru_r1"):
                    g = arg
                    wait_job(act, j)
                    act.wait_ge(s("pooled"), 4)
                    if g == 1:
                        act.wait_ge(s("y_b0_prod"), 4)
                    for q in range(4):
                        nc.scalar.activation(tb[:, q, :], ps[:, bank(j, q), :], ACT.Sigmoid,
                                             bias=col("lru_ba", 4 * g + q)).then_inc(s(f"r{g}"), 1)
                    act.wait_ge(s(f"r{g}"), 4)
                    act.sem_inc(act_read, 1)
                elif kind in ("lru_i0", "lru_i1"):
                    g = arg
                    wait_job(act, j)
                    for q in range(4):
                        nc.scalar.activation(tc[:, q, :], ps[:, bank(j, q), :], ACT.Sigmoid,
                                             bias=col("lru_bx", 4 * g + q)).then_inc(s(f"i{g}"), 1)
                    act.wait_ge(s(f"i{g}"), 4)
                    act.sem_inc(act_read, 1)
                    more(j)
                    act.wait_ge(s("c8_made"), 1)
                    if g == 0:
                        act.wait_ge(s("pooled_lo"), 4)
                    else:
                        act.wait_ge(s("y_b0_lo"), 4)
                    for q in range(4):
                        nc.scalar.activation(td[:, q, :], tb[:, q, :], ACT.Tanh,
                                             scale=c8[:, 8, 4 * g + q:4 * g + q + 1]).then_inc(s(f"t{g}"), 1)
                    more(j)
                    for q in range(4):
                        act.wait_ge(s(f"t{g}"), q + 1)
                        nc.scalar.activation(tb[:, q, :], tb[:, q, :], ACT.Exp,
                                             scale=c8[:, 9, 4 * g + q:4 * g + q + 1]).then_inc(s(f"a{g}"), 1)
                    more(j)
                    for q in range(4):
                        act.wait_ge(s(f"ratio{g}"), q + 1)
                        nc.scalar.activation(td[:, q, :], td[:, q, :], ACT.Sqrt, scale=2.0).then_inc(s(f"root_b{g}"), 1)
                elif kind in ("b_y0", "b_y1"):
                    g = arg // N - 5
                    wait_job(act, j)
                    act.wait_ge(s(f"ratio{g}"), 4)
                    for q in range(4):
                        nc.scalar.activation(ta[:, q, :], ps[:, bank(j, q), :], ACT.Gelu_apprx_tanh).then_inc(s(f"gelu{g}"), 1)
                    act.wait_ge(s(f"gelu{g}"), 4)
                    act.sem_inc(act_read, 1)
                    more(j)
                    hi_of(td, f"y_b{g}_prod", f"y_b{g}_hi", 4 * g)
                elif kind == "b_out":
                    wait_job(act, JOB["gate5"])
                    for q in range(4):
                        act.wait_ge(s("m_sum"), 4 * arg + q + 1)
                        nc.scalar.activation(h_hi[:, 4 * arg + q, :], mt[:, 4 * arg + q, :], ACT.Copy).then_inc(s("m_hi"), 1)

            def root_of(t):
                act.wait_ge(s("x_mid"), t + 1)
                if t:
                    act.wait_ge(s("sq2"), t)
                nc.scalar.activation(flat["ta"][:, 0:D], m_rows[:, t, :], ACT.Square,
                                     accum_out=stat[:, 0, t:t + 1]).then_inc(s("sq2"), 1)
                act.wait_ge(s("ms2"), t + 1)
                nc.scalar.activation(stat[:, 2, t:t + 1], stat[:, 1, t:t + 1], ACT.Sqrt).then_inc(s("root2"), 1)

            def copy_h2_t(t):
                act.wait_ge(s("h2_turned"), t + 1)
                if t >= 2:
                    act.wait_ge(s("logits"), t - 1)
                b0 = bank(JOB["w_o0"], 2 * (t % 2))
                nc.scalar.activation(h2_t[t % 2].rearrange("p k s -> p (k s)"),
                                     ps[:, b0:b0 + 2, :].rearrange("p a b -> p (a b)"), ACT.Copy).then_inc(s("h2_t"), 1)

            def h2_hi(t):
                act.wait_ge(s("h2"), t + 1)
                nc.scalar.activation(rows_hi[:, t, :], h2_nat[t % 2], ACT.Copy).then_inc(s("h2_hi"), 1)

            c0, i0 = MIX_CHUNKS, MIX_SUBS
            root_of(0)
            root_of(1)
            copy_h2_t(0)
            h2_hi(0)
            root_of(2)
            copy_h2_t(1)
            h2_hi(1)
            root_of(3)
            h2_hi(2)
            copy_h2_t(2)
            h2_hi(3)
            copy_h2_t(3)
            for k in range(4):
                moe_hi(i0, 0, c0, k)
            act.wait_ge(s("soft_in"), 1)
            nc.scalar.activation(rt[:, 14, :, 0:NG], rt[:, 13, :, 0:NG], ACT.Exp).then_inc(s("soft_exp"), 1)
            nc.scalar.activation(r1[:, 6, :], r1[:, 5, :], ACT.Exp).then_inc(s("soft_exp"), 1)

            def sel_hi(n, h, used=None):
                act.wait_ge(s("sel_got"), n + 1)
                if used is not None:
                    act.wait_ge(sub_used, used)
                nc.scalar.activation(half_of(h_hi, h), half_bank(h), ACT.Copy).then_inc(s("sel_hi"), 1)

            def silu_of(b, i, turn, first=False):
                act.wait_ge(sub_used, 12 * turn + (i + 4))
                if not first:
                    act.wait_ge(s("hid"), b)
                nc.scalar.activation(silu, ps[:, 0, :], ACT.Silu).then_inc(s("silu"), 1)

            def hid_hi(b):
                act.wait_ge(s("hid_turned"), b + 1)
                nc.scalar.activation(hid_t_hi, ps[:, 1, :].rearrange("p (k s) -> p k s", s=P),
                                     ACT.Copy).then_inc(s("hid_hi"), 1)

            def y_half(n, subs, turn, first=False):
                act.wait_ge(sub_used, 12 * turn + subs)
                if not first:
                    act.wait_ge(s("y_stored"), 16 * n)
                nc.scalar.activation(y_out[:, 0:N], ps[:, 2, :], ACT.Copy).then_inc(s("y_left"), 1)

            sel_hi(0, 0)
            sel_hi(1, 1)
            for k in range(4, 8):
                moe_hi(i0, 0, c0, k)
            silu_of(0, i0, 0, first=True)
            c1, i1 = MIX_CHUNKS + 4, MIX_SUBS + 8
            for k in range(4):
                moe_hi(i1, 0, c1, k)

            def body(e, odd, more_to_come=True, first=False, last=False):
                turn = e - 1
                hid_hi(e - 1)
                for k in range(4, 8):
                    moe_hi(i1, turn, c1, k)
                silu_of(e, i1, turn)
                for k in range(8, 12):
                    moe_hi(i1, turn, c1, k)
                for k in range(4):
                    if more_to_come and odd and k == 0:
                        sel_hi(e + 1, 0, 12 * turn + (i1 + 8))
                    elif more_to_come and odd and k == 2:
                        sel_hi(e + 2, 1)
                    if last and k == 3:
                        hid_hi(e)
                        y_half(e - 1, i1 + 12, turn)
                    moe_hi(i1, e, c1, k)
                if not last:
                    y_half(e - 1, i1 + 12, turn, first)

            body(1, True, first=True)
            with act.Fori(2, NE - 2, 2) as e:
                body(e, False)
                body(e + 1, True)
            body(NE - 2, False)
            body(NE - 1, True, more_to_come=False, last=True)
            act.wait_ge(sub_used, 12 * (NE - 1) + (i1 + 4))
            for half in range(2):
                nc.scalar.activation(y_last[:, half * N:(half + 1) * N], ps[:, 4 + half, :], ACT.Copy).then_inc(s("y_last"), 1)

            act.wait_ge(s("extras_known"), 1)
            n_extra = act.value_load(xtra_i[0:1, 8:9], min_val=0, max_val=EXTRAS)
            with act.If(n_extra > 0):
                with act.Fori(0, EXTRAS) as j:
                    with act.If(n_extra > j):
                        b = NE + j
                        cx, ix = XTRA_BASE
                        sel_hi(NE + 2 * j, 0)
                        sel_hi(NE + 2 * j + 1, 1)
                        for k in range(8):
                            moe_hi(ix, j, cx, k)
                        silu_of(b, ix, j)
                        for k in range(8, 12):
                            moe_hi(ix, j, cx, k)
                        hid_hi(b)
                        y_half(NE - 1 + j, ix + 12, j)

            act.wait_ge(s("table_in"), 1)
            nc.scalar.activation(stat[:, 5, 0:1], eps_col[:, :], ACT.Sqrt).then_inc(s("table_in"), 1)
            for t in range(TT):
                act.wait_ge(s("merged"), t + 1)
                if t:
                    act.wait_ge(s("sq3"), t)
                nc.scalar.activation(flat["tb"][:, 0:D], m_rows[:, t, :], ACT.Square,
                                     accum_out=stat[:, 4, t:t + 1]).then_inc(s("sq3"), 1)
                act.wait_ge(s("sq3"), t + 1)
                nc.scalar.activation(stat[:, 6, t:t + 1], stat[:, 4, t:t + 1], ACT.Sqrt, scale=1.0 / D,
                                     bias=eps_col[:, :]).then_inc(s("root3"), 1)

        @block.vector
        def _(dve):
            made = [0]
            steps = [0]
            V = nc.vector

            def link(ins):
                steps[0] += 1
                ins.then_inc(s("dve_step"), 1)
                dve.wait_ge(s("dve_step"), steps[0])

            def lo_sub(slot, src, n):
                V.tensor_tensor(w_lo[:, slot, 0:n, :], src, w_hi[:, slot, 0:n, :], SUB).then_inc(lo_made, 1)

            def split_next():
                i = made[0]
                dve.wait_ge(hi_made, i + 1)
                t, n = mix_sub(i)
                lo_sub(i % SUB_SLOTS, t, n)
                made[0] += 1

            def split_for(j):
                while made[0] < subs_by(j):
                    split_next()

            def more(j):
                if made[0] < most_by(j):
                    split_next()

            def moe_lo(i0, turn, c0, k):
                dve.wait_ge(hi_made, 12 * turn + (i0 + k + 1))
                c = c0 + k // 2
                lo_sub((i0 + k) % SUB_SLOTS, raw[:, c % RAW_SLOTS, 2 * (k % 2):2 * (k % 2) + 2, :], 2)

            def square(t):
                dve.wait_ge(s(f"x_in{t}"), 16)
                V.tensor_tensor_reduce(out=flat["tb"][:, t // 2 * D:(t // 2 + 1) * D], in0=m_rows[:, t, :], in1=m_rows[:, t, :],
                                       scale=1.0, scalar=0.0, op0=MUL, op1=ADD,
                                       accum_out=stat[:, 0, t:t + 1]).then_inc(s(f"sq1_{t}"), 1)

            def scale(t):
                dve.wait_ge(s("root1"), t + 1)
                link(V.reciprocal(stat[:, 3, t:t + 1], stat[:, 2, t:t + 1]))
                V.tensor_scalar(m_rows[:, t, :], m_rows[:, t, :], stat[:, 3, t:t + 1], None, MUL).then_inc(s("x_scaled"), 1)

            scale(0)
            square(1)
            scale(1)
            scale(2)
            square(3)
            scale(3)
            split_next()
            dve.wait_ge(s("rows_turned"), 1)
            V.tensor_copy(cols[:, :], ps[:, 7, 0:NROWS]).then_inc(s("cols_made"), 1)
            split_next()
            for k in range(KD):
                if k == 4 or k == 6:
                    split_next()
                dve.wait_ge(s("h_hi"), k + 1)
                V.scalar_tensor_tensor(out=h_lo[:, k, :], in0=ps[:, k, :], scalar=col("norm1_g", k),
                                       in1=h_hi[:, k, :], op0=MUL, op1=SUB).then_inc(s("h_lo"), 1)
            dve.wait_ge(s("iotas"), 10)
            for g, w in enumerate(WINDOWS):
                link(V.tensor_scalar(inv_cnt[:, g, :], inv_cnt[:, g, :], float(w), None, ALU.min))
            link(V.reciprocal(inv_cnt[:, :, :], inv_cnt[:, :, :]))
            dve.wait_ge(s("exp_lam"), 1)
            lam = cols[:, ROWS["lru_lambda"]:ROWS["lru_lambda"] + KD]
            e_, z, z2, q_ = c8[:, 1, :], c8[:, 2, :], c8[:, 3, :], c8[:, 4, :]
            link(V.tensor_scalar(z, e_, 2.0, None, ADD))
            link(V.reciprocal(z, z))
            link(V.tensor_tensor(z, z, e_, MUL))
            link(V.tensor_tensor(z2, z, z, MUL))
            link(V.tensor_scalar(q_, z2, 1.0 / 17, None, MUL))
            for d in (15, 13, 11, 9, 7, 5, 3):
                link(V.scalar_tensor_tensor(out=q_, in0=q_, scalar=1.0 / d, in1=z2, op0=ADD, op1=MUL))
            link(V.scalar_tensor_tensor(out=q_, in0=q_, scalar=1.0, in1=z, op0=ADD, op1=MUL))
            link(V.tensor_scalar(c8[:, 5, :], lam, -1.0, 0.0, MUL, ALU.max))
            link(V.scalar_tensor_tensor(out=c8[:, 6, :], in0=q_, scalar=2.0, in1=c8[:, 5, :], op0=MUL, op1=ADD))
            link(V.tensor_scalar(c8[:, 8, :], c8[:, 6, :], 8.0, None, MUL))
            V.tensor_scalar(c8[:, 9, :], c8[:, 6, :], -8.0, None, MUL).then_inc(s("c8_made"), 1)

            def lo_of(src, name_hi, name_out, y0):
                for q in range(4):
                    dve.wait_ge(s(name_hi), q + 1)
                    V.tensor_tensor(y_lo[:, y0 + q, :], src[:, q, :], y_hi[:, y0 + q, :], SUB).then_inc(s(name_out), 1)

            for j, (kind, arg, n) in enumerate(JOBS):
                split_for(j)
                title = TITLES[j]
                if kind == "a_x":
                    wait_job(dve, j)
                    for q in range(4):
                        dve.wait_ge(s("a_c"), q + 1)
                        V.tensor_tensor(tc[:, q, :], ps[:, bank(j, q), :], tb[:, q, :], MUL).then_inc(s("a_u"), 1)
                    dve.wait_ge(s("a_u"), 4)
                    dve.sem_inc(dve_read, 1)
                    for q in range(4):
                        V.tensor_scalar(td[:, q, :], tc[:, q, :], col("conv_a_w", 8 + q), None, MUL).then_inc(s("conv_a"), 1)
                    for tap in (1, 2):
                        more(j)
                        for q in range(4):
                            dve.wait_ge(s("conv_a"), 4 * (tap - 1) + q + 1)
                            V.scalar_tensor_tensor(out=td[:, q, tap:], in0=tc[:, q, 0:SEQ - tap],
                                                   scalar=col("conv_a_w", 4 * (2 - tap) + q), in1=td[:, q, tap:],
                                                   op0=MUL, op1=ADD).then_inc(s("conv_a"), 1)
                elif kind == "a_b":
                    wait_job(dve, j)
                    dve.wait_ge(s("conv_a"), 12)
                    for q in range(4):
                        V.tensor_tensor(ta[:, q, :], ps[:, bank(j, q), :], td[:, q, :], MUL).then_inc(s("y_a"), 1)
                    dve.wait_ge(s("y_a"), 4)
                    dve.sem_inc(dve_read, 1)
                    lo_of(ta, "y_a_hi", "y_a_lo", 0)
                elif kind == "c_u":
                    dve.wait_ge(s("c_u"), 4)
                    for q, w in enumerate(WINDOWS):
                        src, step = tb, 1
                        for lv in range(q + 1):
                            dst = (td, tc)[(q - lv) % 2]
                            V.tensor_copy(dst[:, q, 0:step], src[:, q, 0:step])
                            link(V.tensor_tensor(dst[:, q, step:], src[:, q, step:], src[:, q, 0:SEQ - step], ADD))
                            src, step = dst, 2 * step
                        link(V.tensor_tensor(tc[:, q, 0:16], td[:, q, 0:16], inv_cnt[:, q, :], MUL))
                        link(V.scalar_tensor_tensor(out=td[:, q, 16:], in0=td[:, q, 16:], scalar=1.0 / w, in1=tb[:, q, 16:],
                                                    op0=MUL, op1=SUB))
                        V.tensor_tensor(td[:, q, 0:16], tc[:, q, 0:16], tb[:, q, 0:16], SUB).then_inc(s("pooled"), 1)
                    lo_of(td, "pooled_hi", "pooled_lo", 4)
                elif kind == "pool":
                    wait_job(dve, j)
                    for q in range(4):
                        dve.wait_ge(s("y_c_hi"), q + 1)
                        V.scalar_tensor_tensor(out=y_lo[:, 4 + q, :], in0=ps[:, bank(j, q), :], scalar=col("pool_scale", q),
                                               in1=y_hi[:, 4 + q, :], op0=MUL, op1=SUB).then_inc(s("y_c_lo"), 1)
                    dve.wait_ge(s("y_c_lo"), 4)
                    dve.sem_inc(dve_read, 1)
                elif kind in ("a_out", "c_out", "b_out"):
                    wait_job(dve, j)
                    g = [t for t in TITLES if "_out" in t].index(title)
                    sig = gate_of(g)
                    dve.wait_ge(s("gate"), 4 * g + 4)
                    for q in range(4):
                        o = mt[:, 4 * arg + q, :]
                        if kind == "a_out":
                            V.tensor_tensor(o, ps[:, bank(j, q), :], sig[:, q, :], MUL).then_inc(s("gated"), 1)
                        else:
                            V.tensor_tensor(sig[:, q, :], ps[:, bank(j, q), :], sig[:, q, :], MUL).then_inc(s("gate_prod"), 1)
                    if kind == "a_out":
                        dve.wait_ge(s("gated"), 4 * g + 4)
                        dve.sem_inc(dve_read, 1)
                    else:
                        base = 4 * (g - 2)
                        dve.wait_ge(s("gate_prod"), base + 4)
                        dve.sem_inc(dve_read, 1)
                        for q in range(4):
                            o = mt[:, 4 * arg + q, :]
                            ins = V.tensor_tensor(o, o, sig[:, q, :], ADD)
                            ins.then_inc(s("gated"), 1)
                            if kind == "b_out":
                                dve.wait_ge(s("gated"), 4 * g + q + 1)
                                dve.sem_inc(s("m_sum"), 1)
                    if kind == "b_out":
                        for q in range(4):
                            k = 4 * arg + q
                            dve.wait_ge(s("m_hi"), k + 1)
                            V.tensor_tensor(h_lo[:, k, :], mt[:, k, :], h_hi[:, k, :], SUB).then_inc(s("m_lo"), 1)
                        dve.wait_ge(s("m_lo"), 4 * arg + 4)
                        dve.sem_inc(s("m_split"), 1)
                elif kind in ("b_x0", "b_x1"):
                    g = arg // N - 3
                    wait_job(dve, j)
                    for tap in (1, 2, 3):
                        for q in range(4):
                            c = 4 * g + q
                            if tap == 1:
                                dve.wait_ge(s(f"x_b{g}_tap"), q + 1)
                            else:
                                dve.wait_ge(s(f"x_b{g}_sum"), 4 * (tap - 2) + q + 1)
                            ins = V.scalar_tensor_tensor(out=ta[:, q, tap:], in0=ps[:, bank(j, q), 0:SEQ - tap],
                                                         scalar=col("conv_b_w", (3 - tap) * KD + c), in1=ta[:, q, tap:],
                                                         op0=MUL, op1=ADD)
                            ins.then_inc(s(f"x_b{g}") if tap == 3 else s(f"x_b{g}_sum"), 1)
                    dve.wait_ge(s(f"x_b{g}"), 4)
                    dve.sem_inc(dve_read, 1)
                    lo_of(ta, f"x_b{g}_hi", f"x_b{g}_lo", 4 * g)
                elif kind in ("lru_i0", "lru_i1"):
                    g = arg
                    for q in range(4):
                        dve.wait_ge(s(f"i{g}"), q + 1)
                        V.tensor_tensor(tc[:, q, :], tc[:, q, :], ta[:, q, :], MUL).then_inc(s(f"ix{g}"), 1)
                    more(j)
                    for q in range(4):
                        dve.wait_ge(s(f"t{g}"), q + 1)
                        dve.wait_ge(s(f"ix{g}"), q + 1)
                        link(V.tensor_scalar(ta[:, q, :], td[:, q, :], 1.0, None, ADD))
                        link(V.reciprocal(ta[:, q, :], ta[:, q, :]))
                        V.tensor_tensor(td[:, q, :], td[:, q, :], ta[:, q, :], MUL).then_inc(s(f"ratio{g}"), 1)
                        if q % 2 == 0:
                            more(j)
                    for q in range(4):
                        dve.wait_ge(s(f"a{g}"), q + 1)
                        dve.wait_ge(s(f"root_b{g}"), q + 1)
                        link(V.tensor_tensor(td[:, q, :], td[:, q, :], tc[:, q, :], MUL))
                        V.tensor_tensor_scan(tc[:, q, :], tb[:, q, :], td[:, q, :], 0.0, MUL, ADD).then_inc(s(f"y_b{g}_scan"), 1)
                        if q in (1, 2):
                            more(j)
                elif kind in ("b_y0", "b_y1"):
                    g = arg // N - 5
                    for q in range(4):
                        dve.wait_ge(s(f"y_b{g}_scan"), q + 1)
                        dve.wait_ge(s(f"gelu{g}"), q + 1)
                        V.tensor_tensor(td[:, q, :], tc[:, q, :], ta[:, q, :], MUL).then_inc(s(f"y_b{g}_prod"), 1)
                    lo_of(td, f"y_b{g}_hi", f"y_b{g}_lo", 4 * g)
                elif kind == "w_o" and arg == 0:
                    wait_job(dve, j)
                    dve.wait_ge(s("x_again"), 16)
                    for t in range(TT):
                        o = m_rows[:, t, 0:N]
                        V.tensor_tensor(o, o, ps[:, bank(j, t), :], ADD).then_inc(s("x_mid0"), 1)
                    dve.wait_ge(s("x_mid0"), 4)
                    dve.sem_inc(dve_read, 1)

            def h2_lo(t):
                dve.wait_ge(s("h2_hi"), t + 1)
                V.tensor_tensor(rows_lo[:, t, :], h2_nat[t % 2], rows_hi[:, t, :], SUB).then_inc(s("h2_lo"), 1)

            j = JOB["w_o1"]
            dve.wait_ge(s("norm_rows"), 32)
            for t in range(TT):
                if t < TT - 1:
                    dve.wait_ge(s("w_o_tile"), t + 1)
                else:
                    dve.wait_ge(sub_used, MIX_SUBS)
                o = m_rows[:, t, N:D]
                V.tensor_tensor(o, o, ps[:, bank(j, t), :], ADD).then_inc(s("x_mid"), 1)
                dve.wait_ge(s("sq2"), t + 1)
                V.tensor_scalar(stat[:, 1, t:t + 1], stat[:, 0, t:t + 1], 1.0 / D, EPS, MUL, ADD).then_inc(s("ms2"), 1)
                dve.wait_ge(s("root2"), t + 1)
                link(V.reciprocal(stat[:, 3, t:t + 1], stat[:, 2, t:t + 1]))
                if t >= 2:
                    dve.wait_ge(s("h2_turned"), t - 1)
                    dve.wait_ge(s("h2_hi"), t - 1)
                V.scalar_tensor_tensor(out=h2_nat[t % 2], in0=m_rows[:, t, :], scalar=stat[:, 3, t:t + 1], in1=norm2_row,
                                       op0=MUL, op1=MUL).then_inc(s("h2"), 1)
                if t:
                    h2_lo(t - 1)
            c0, i0 = MIX_CHUNKS, MIX_SUBS
            h2_lo(TT - 1)
            moe_lo(i0, 0, c0, 0)
            dve.wait_ge(s("router_in"), 64)
            lg, eg = logit[:, :, 0:NG], logit[:, :, NG:20]
            for t in range(TT):
                dve.wait_ge(s("logits"), t + 1)
                ins = V.tensor_tensor(logit[:, t, :], ps[:, bank(JOB["w_o1"], t), 0:20], b_r[:, :], ADD)
            link(ins)
            e_no, grp_of, g_no = rc[:, 0, :, :], rc[:, 1, :, :], rc[:, 2, :, 0:NG]

            def wide(v, n):
                return v.unsqueeze(2).to_broadcast([P, TT, n])

            link(V.tensor_reduce(r1[:, 0, :], lg, AX_X, ALU.max))
            link(V.tensor_tensor(rt[:, 6, :, 0:NG], lg, wide(r1[:, 0, :], NG), ALU.is_equal))
            link(V.tensor_tensor(rt[:, 6, :, 0:NG], rt[:, 6, :, 0:NG], g_no, MUL))
            link(V.tensor_reduce(r1[:, 1, :], rt[:, 6, :, 0:NG], AX_X, ALU.min))
            link(V.tensor_tensor(rt[:, 7, :, :], grp_of, wide(r1[:, 1, :], NE), ALU.is_equal))
            link(V.tensor_scalar(rt[:, 8, :, :], rt[:, 7, :, :], -1.0, BIG, ADD, MUL))
            link(V.tensor_tensor(rt[:, 8, :, :], rt[:, 8, :, :], eg, ADD))
            for k in range(2):
                if k:
                    link(V.scalar_tensor_tensor(out=rt[:, 8, :, :], in0=rt[:, 10, :, :], scalar=-3.0 * BIG, in1=rt[:, 8, :, :],
                                                op0=MUL, op1=ADD))
                link(V.tensor_reduce(r1[:, 2 + k, :], rt[:, 8, :, :], AX_X, ALU.max))
                link(V.tensor_tensor(rt[:, 9, :, :], rt[:, 8, :, :], wide(r1[:, 2 + k, :], NE), ALU.is_equal))
                link(V.tensor_tensor(rt[:, 9, :, :], rt[:, 9, :, :], e_no, MUL))
                link(V.tensor_reduce(r1[:, 4, :], rt[:, 9, :, :], AX_X, ALU.min))
                link(V.tensor_tensor(rt[:, 10 + k, :, :], e_no, wide(r1[:, 4, :], NE), ALU.is_equal))
            V.tensor_tensor(routed16[:, :, :], rt[:, 10, :, :], rt[:, 11, :, :], ADD).then_inc(s("routed"), 1)
            V.tensor_tensor(rt[:, 13, :, 0:NG], lg, wide(r1[:, 0, :], NG), SUB)
            V.tensor_tensor(r1[:, 5, :], r1[:, 3, :], r1[:, 2, :], SUB).then_inc(s("soft_in"), 1)
            dve.wait_ge(s("ranked"), 1)
            rb = bank(JOB["w_o0"], 3)
            link(V.tensor_copy(ranks, ps[:, rb, 0:(TT + 1) * NE]))
            rank, count = ranks[:, 0:TT * NE].rearrange("p (t e) -> p t e", e=NE), ranks[:, TT * NE:(TT + 1) * NE]
            link(V.scalar_tensor_tensor(out=rt[:, 12, :, :], in0=rank, scalar=1.0, in1=routed16[:, :, :], op0=ADD, op1=MUL))
            link(V.tensor_scalar(slot_tab[:, 0:NE, :].rearrange("p e t -> p t e"), rt[:, 12, :, :], -1.0, None, ADD))

            def slots(b, halves):
                if halves is not None:
                    dve.wait_ge(s("sel_got"), halves)
                V.tensor_tensor(one_hot.rearrange("p t (c s) -> p t c s", s=P),
                                slot_iota[:, :].unsqueeze(1).unsqueeze(1).to_broadcast([P, TT, 2, P]),
                                slot_tab[:, bass.ds(b, 2), :].rearrange("p c t -> p t c").unsqueeze(3).to_broadcast([P, TT, 2, P]),
                                ALU.is_equal).then_inc(s("slots"), 1)

            slots(0, None)
            link(V.tensor_scalar(cnt[:, 1, :], count, float(P), None, ALU.is_gt))
            for k in range(1, 4):
                moe_lo(i0, 0, c0, k)
            for k in (2, 3):
                link(V.scalar_tensor_tensor(out=cnt[:, 1, :], in0=count, scalar=float(k * P), in1=cnt[:, 1, :],
                                            op0=ALU.is_gt, op1=ADD))
            V.memset(cnt[:, 3, :], 1.0)
            link(V.tensor_copy(cnt[:, 4, :], cnt[:, 1, :]))
            link(V.tensor_tensor_scan(cnt[:, 2, :], cnt[:, 3, :], cnt[:, 4, :], 0.0, MUL, ADD))
            link(V.tensor_tensor(cnt[:, 5, :], cnt[:, 2, :], cnt[:, 1, :], SUB))
            link(V.scalar_tensor_tensor(out=cnt[:, 5, :], in0=cnt[:, 5, :], scalar=float(P), in1=cnt[:, 0, :], op0=MUL, op1=ADD))
            link(V.tensor_scalar(rt[:, 12, :, :], rank, float(P), None, ALU.is_ge))
            link(V.tensor_tensor(rt[:, 12, :, :], rt[:, 12, :, :], cnt[:, 5, :].unsqueeze(1).to_broadcast([P, TT, NE]), MUL))
            link(V.tensor_tensor(rt[:, 12, :, :], rt[:, 12, :, :], rc[:, 3, :, :], ADD))
            link(V.tensor_tensor(rt[:, 12, :, :], rt[:, 12, :, :], rank, ADD))
            for k in range(2):
                link(V.tensor_tensor(rt[:, 9, :, :], rt[:, 12, :, :], rt[:, 10 + k, :, :], MUL))
                link(V.tensor_reduce(pos_rel[:, k, :], rt[:, 9, :, :], AX_X, ADD))

            def sel_lo(n, h):
                dve.wait_ge(s("sel_hi"), n + 1)
                V.tensor_tensor(half_of(h_lo, h), half_bank(h), half_of(h_hi, h), SUB).then_inc(s("sel_lo"), 1)

            def hid_of(b, i, turn, first=False):
                dve.wait_ge(sub_used, 12 * turn + (i + 8))
                dve.wait_ge(s("silu"), b + 1)
                if not first:
                    dve.wait_ge(s("hid_turned"), b)
                V.tensor_tensor(hid, ps[:, 1, :], silu, MUL).then_inc(s("hid"), 1)

            def hid_lo(b):
                dve.wait_ge(s("hid_hi"), b + 1)
                V.tensor_tensor(hid_t_lo, ps[:, 1, :].rearrange("p (k s) -> p k s", s=P), hid_t_hi, SUB).then_inc(s("hid_lo"), 1)

            def y_half(n, subs, turn, first=False):
                dve.wait_ge(sub_used, 12 * turn + subs)
                if not first:
                    dve.wait_ge(s("y_stored"), 16 * n)
                V.tensor_copy(y_out[:, N:D], ps[:, 3, :]).then_inc(s("y_right"), 1)

            link(V.tensor_tensor(pos_two[:, 0, :], pos_rel[:, 0, :], pos_rel[:, 1, :], ALU.min))
            link(V.tensor_tensor(pos_two[:, 1, :], pos_rel[:, 0, :], pos_rel[:, 1, :], ALU.max))
            link(V.tensor_copy(pos_i[:, :, :], pos_two[:, :, :]))
            sel_lo(0, 0)
            sel_lo(1, 1)
            slots(2, 2)
            for k in range(2):
                v, w = rt[:, k, :, 0:EXTRAS + 2].rearrange("p t j -> p j t"), rt[:, 2 + k, :, 0:EXTRAS + 2].rearrange("p t j -> p j t")
                link(V.tensor_tensor(v, pos_rel[:, k, :].unsqueeze(1).to_broadcast([P, EXTRAS + 2, TT]), xtra_at[:, :, :], ADD))
                link(V.tensor_scalar(w, v, float(P), None, ALU.is_lt))
                link(V.scalar_tensor_tensor(out=w, in0=v, scalar=1.0, in1=w, op0=ADD, op1=MUL))
            link(V.tensor_tensor(v, rt[:, 2, :, 0:EXTRAS + 2].rearrange("p t j -> p j t"), w, ALU.max))
            link(V.tensor_scalar(slot_tab[:, NE:NE + EXTRAS + 2, :], v, -1.0, None, ADD))
            link(V.tensor_tensor(xtra[:, :, :], cnt[0:1, 2, :].unsqueeze(1).to_broadcast([1, 8, NE]), xtra[:, :, :], ALU.is_le))
            link(V.tensor_reduce(xtra_n[:, :], xtra[:, :, :], AX_X, ADD))
            link(V.tensor_copy(xtra_i[:, 0:8], xtra_n[:, :]))
            V.tensor_copy(xtra_i[:, 8:9], cnt[0:1, 2, NE - 1:NE]).then_inc(s("extras_known"), 1)
            c1, i1 = MIX_CHUNKS + 4, MIX_SUBS + 8
            for k in range(4, 8):
                moe_lo(i0, 0, c0, k)
            dve.wait_ge(s("soft_exp"), 2)
            link(V.tensor_reduce(r1[:, 7, :], rt[:, 14, :, 0:NG], AX_X, ADD))
            link(V.tensor_scalar(r1[:, 8, :], r1[:, 6, :], 1.0, None, ADD))
            link(V.tensor_tensor(r1[:, 8, :], r1[:, 8, :], r1[:, 7, :], MUL))
            link(V.reciprocal(r1[:, 9, :], r1[:, 8, :]))
            link(V.tensor_tensor(r1[:, 10, :], r1[:, 9, :], r1[:, 6, :], MUL))
            link(V.tensor_tensor(r1[:, 0, :], pos_rel[:, 0, :], pos_rel[:, 1, :], ALU.is_lt))
            link(V.tensor_scalar(r1[:, 1, :], r1[:, 0, :], -1.0, 1.0, MUL, ADD))
            for row, a, b in ((2, 0, 1), (3, 1, 0)):
                link(V.tensor_tensor(r1[:, 4, :], r1[:, 9, :], r1[:, a, :], MUL))
                link(V.tensor_tensor(r1[:, 5, :], r1[:, 10, :], r1[:, b, :], MUL))
                link(V.tensor_tensor(r1[:, row, :], r1[:, 4, :], r1[:, 5, :], ADD))

            hid_of(0, i0, 0, first=True)
            for k in range(4):
                moe_lo(i1, 0, c1, k)

            def body(e, odd, more_to_come=True, first=False, last=False):
                turn = e - 1
                hid_lo(e - 1)
                for k in range(4, 8):
                    moe_lo(i1, turn, c1, k)
                if more_to_come and odd:
                    slots(e + 3, e + 3)
                for k in range(8, 12):
                    if k == 11:
                        hid_of(e, i1, turn)
                    moe_lo(i1, turn, c1, k)
                for k in range(4):
                    if more_to_come and odd and k % 2 == 0:
                        sel_lo(e + 1 + k // 2, k // 2)
                    if last and k == 2:
                        hid_lo(e)
                        y_half(e - 1, i1 + 12, turn)
                    moe_lo(i1, e, c1, k)
                if not last:
                    y_half(e - 1, i1 + 12, turn, first)

            body(1, True, first=True)
            with dve.Fori(2, NE - 2, 2) as e:
                body(e, False)
                body(e + 1, True)
            body(NE - 2, False)
            body(NE - 1, True, more_to_come=False, last=True)

            def merge_first():
                for t in range(TT):
                    o = m_rows[:, t, :]
                    dve.wait_ge(s(f"y_got{t}0"), 16)
                    V.scalar_tensor_tensor(out=o, in0=y_got[t][0], scalar=r1[:, 2, t:t + 1], in1=o,
                                           op0=MUL, op1=ADD).then_inc(s("merged_first"), 1)

            dve.wait_ge(s("extras_known"), 1)
            n_extra = dve.value_load(xtra_i[0:1, 8:9], min_val=0, max_val=EXTRAS)
            with dve.If(n_extra < 1):
                merge_first()
            with dve.If(n_extra > 0):
                with dve.Fori(0, EXTRAS) as j:
                    with dve.If(n_extra > j):
                        b = NE + j
                        cx, ix = XTRA_BASE
                        sel_lo(NE + 2 * j, 0)
                        sel_lo(NE + 2 * j + 1, 1)
                        slots(b + 1, NE + 2 * j + 2)
                        for k in range(8):
                            moe_lo(ix, j, cx, k)
                        hid_of(b, ix, j)
                        for k in range(8, 12):
                            moe_lo(ix, j, cx, k)
                        hid_lo(b)
                        y_half(NE - 1 + j, ix + 12, j)

            with dve.If(n_extra > 0):
                merge_first()

            def merge(t):
                o = m_rows[:, t, :]
                dve.wait_ge(s("merged_first"), t + 1)
                dve.wait_ge(s(f"y_got{t}1"), 16)
                V.scalar_tensor_tensor(out=o, in0=y_got[t][1], scalar=r1[:, 3, t:t + 1], in1=o,
                                       op0=MUL, op1=ADD).then_inc(s("merged"), 1)

            def final_of(t):
                dve.wait_ge(s("root3"), t + 1)
                link(V.reciprocal(stat[:, 7, t:t + 1], stat[:, 6, t:t + 1]))
                V.scalar_tensor_tensor(out=y_got[t][0], in0=m_rows[:, t, :], scalar=stat[:, 7, t:t + 1], in1=final_row,
                                       op0=MUL, op1=MUL).then_inc(s("final_rows"), 1)

            for t in range(TT):
                merge(t)
                if t:
                    final_of(t - 1)
            final_of(TT - 1)

        @block.tensor
        def _(pe):
            T = nc.tensor

            def three(o, a_hi, a_lo, b_hi, b_lo, start, stop):
                T.matmul(o, a_hi, b_hi, start=start, stop=False)
                T.matmul(o, a_hi, b_lo, start=False, stop=False)
                return T.matmul(o, a_lo, b_hi, start=False, stop=stop)

            def turn_x(t, k):
                return T.transpose(ps[:, k, t * P:(t + 1) * P], m_rows[:, t, k * P:(k + 1) * P], ident[:, :])

            pe.wait_ge(s("ident_made"), 1)
            for t in range(TT):
                if t == TT - 1:
                    pe.wait_ge(s("rows_in"), 4 * 16)
                    pe.wait_ge(s("more_rows_in"), 4 * 16)
                    T.transpose(ps[:, 7, 0:NROWS], rows[:, :], ident[0:NROWS, 0:NROWS]).then_inc(s("rows_turned"), 1)
                pe.wait_ge(s("x_scaled"), t + 1)
                for k in range(KD - 1):
                    ins = turn_x(t, k)
                    if t == TT - 1:
                        ins.then_inc(s("x_turned"), 1)
            pe.wait_ge(s("cols_made"), 1)
            for t in range(TT):
                ins = turn_x(t, KD - 1)
            ins.then_inc(s("x_turned"), 1)

            def sub_ready(i):
                pe.wait_ge(lo_made, i + 1)

            def turn_h2(t):
                pe.wait_ge(s("h2"), t + 1)
                if t == 0:
                    pe.wait_ge(dve_read, dve_reads(JOB["w_o0"]))
                if t >= 2:
                    pe.wait_ge(s("h2_t"), t - 1)
                for k in range(KD):
                    ins = T.transpose(ps[:, bank(JOB["w_o0"], 2 * (t % 2) + k // 4), (k % 4) * P:(k % 4 + 1) * P],
                                      h2_nat[t % 2][:, k * P:(k + 1) * P], ident[:, :])
                ins.then_inc(s("h2_turned"), 1)

            def route(t):
                if t == 0:
                    pe.wait_ge(s("router_in"), 64)
                pe.wait_ge(s("h2_t"), t + 1)
                pe.wait_ge(s("x_mid"), t + 1)
                for k in range(KD):
                    ins = T.matmul(ps[:, bank(JOB["w_o1"], t), 0:20], h2_t[t % 2][:, k, :], w_r[:, k, :],
                                   start=(k == 0), stop=(k == KD - 1))
                ins.then_inc(s("logits"), 1)
            sub = [0]
            for j, (kind, arg, n) in enumerate(JOBS):
                if j < 2:
                    pe.wait_ge(s("h_lo"), 4 * j + 4)
                else:
                    if act_reads(j - 2):
                        pe.wait_ge(act_read, act_reads(j - 2))
                    if dve_reads(j - 2):
                        pe.wait_ge(dve_read, dve_reads(j - 2))
                if kind in ("lru_r0", "lru_i0", "lru_r1", "lru_i1", "pool"):
                    if kind == "pool":
                        pe.wait_ge(s("pooled_lo"), 4)
                        y0 = 4
                    else:
                        pe.wait_ge(s(f"x_b{arg}_lo"), 4)
                        y0 = 4 * arg
                    if kind[:5] != "lru_i":
                        sub_ready(sub[0])
                        sub[0] += 1
                    slot = (sub[0] - 1) % SUB_SLOTS
                    a = 1 if kind[:5] == "lru_i" else 0
                    for q in range(4):
                        c = slice(q * P, (q + 1) * P)
                        ins = three(ps[:, bank(j, q), :], w_hi[:, slot, a, c], w_lo[:, slot, a, c],
                                    y_hi[:, y0 + q, :], y_lo[:, y0 + q, :], True, True)
                    ins.then_inc(s("lru_r_done") if kind[:5] == "lru_r" else sub_used, 1)
                    continue
                if kind == "w_o" and arg == 1:
                    for t in range(TT):
                        for i in range(4):
                            if t == 0:
                                sub_ready(sub[0] + i)
                            for k in range(2):
                                kk = 2 * i + k
                                c = slice(t * P, (t + 1) * P)
                                slot = (sub[0] + i) % SUB_SLOTS
                                ins = three(ps[:, bank(j, t), :], h_hi[:, kk, c], h_lo[:, kk, c],
                                            w_hi[:, slot, k, :], w_lo[:, slot, k, :], kk == 0, kk == KD - 1)
                            if t == TT - 1:
                                ins.then_inc(sub_used, 1)
                        if t < TT - 1:
                            ins.then_inc(s("w_o_tile"), 1)
                        if t == 1:
                            turn_h2(0)
                        elif t == 2:
                            route(0)
                            turn_h2(1)
                    sub[0] += 4
                    route(1)
                    turn_h2(2)
                    turn_h2(3)
                    route(2)
                    route(3)
                    continue
                if kind == "a_out":
                    pe.wait_ge(s("y_a_lo"), 4)
                elif kind == "c_out":
                    pe.wait_ge(s("y_c_lo"), 4)
                elif kind == "b_out":
                    pe.wait_ge(s("y_b0_lo"), 4)
                rhs_hi, rhs_lo, y0 = (y_hi, y_lo, 4 if kind == "c_out" else 0) if "_out" in kind else (h_hi, h_lo, 0)
                for i in range(n):
                    sub_ready(sub[0])
                    if j == 0 and i > 1:
                        pe.wait_ge(s("h_lo"), 2 * i + 2)
                    if kind == "b_out" and i == 2:
                        pe.wait_ge(s("y_b1_lo"), 4)
                    if kind == "w_o":
                        pe.wait_ge(s("m_lo"), 2 * i + 2)
                    slot = sub[0] % SUB_SLOTS
                    for k in range(2):
                        kk = 2 * i + k
                        first, last = kk == 0, kk == 2 * n - 1
                        for q in range(4):
                            c = slice(q * P, (q + 1) * P)
                            if kind == "w_o":
                                ins = three(ps[:, bank(j, q), :], h_hi[:, kk, c], h_lo[:, kk, c],
                                            w_hi[:, slot, k, :], w_lo[:, slot, k, :], first, last)
                            else:
                                ins = three(ps[:, bank(j, q), :], w_hi[:, slot, k, c], w_lo[:, slot, k, c],
                                            rhs_hi[:, y0 + kk, :], rhs_lo[:, y0 + kk, :], first, last)
                    ins.then_inc(sub_used, 1)
                    sub[0] += 1

            pe.wait_ge(s("routed"), 1)
            rb = bank(JOB["w_o0"], 3)
            for t in range(TT + 1):
                o = ps[:, rb, t * NE:(t + 1) * NE]
                for u in range(min(t + 1, TT)):
                    ins = T.matmul(o, ltri[:, :] if u == t else ones16[:, :], routed16[:, u, :],
                                   start=(u == 0), stop=(u == min(t, TT - 1)))
            ins.then_inc(s("ranked"), 1)

            def gather(n, h, pairs=None, first=False):
                if pairs is not None:
                    pe.wait_ge(s("slots"), pairs)
                if isinstance(n, int) and n == 0:
                    pe.wait_ge(s("h2_lo"), TT)
                if not first:
                    pe.wait_ge(s("sel_lo"), n - 1)
                for k in range(4):
                    o = half_bank(h)[:, k, :]
                    c = slice((4 * h + k) * P, (4 * h + k + 1) * P)
                    for t in range(TT):
                        T.matmul(o, rows_hi[:, t, c], one_hot[:, t, :], start=(t == 0), stop=False)
                        ins = T.matmul(o, rows_lo[:, t, c], one_hot[:, t, :], start=False, stop=(t == TT - 1))
                ins.then_inc(s("sel_got"), 1)

            def turn_hid(b, first=False):
                pe.wait_ge(s("hid"), b + 1)
                if not first:
                    pe.wait_ge(s("hid_lo"), b)
                for k in range(4):
                    ins = T.transpose(ps[:, 1, k * P:(k + 1) * P], hid[:, k * P:(k + 1) * P], ident[:, :])
                ins.then_inc(s("hid_turned"), 1)

            def up(i0, turn, k0, o, odd, halves=None):
                at = slice(odd * P, odd * P + P)
                for i in range(4):
                    if halves is not None and i % 2 == 0:
                        pe.wait_ge(s("sel_lo"), halves - 1 + i // 2)
                    pe.wait_ge(lo_made, 12 * turn + (i0 + k0 + i + 1))
                    slot = (i0 + k0 + i) % SUB_SLOTS
                    for k in range(2):
                        kk = 2 * i + k
                        ins = three(o, h_hi[:, kk, at], h_lo[:, kk, at], w_hi[:, slot, k, :], w_lo[:, slot, k, :],
                                    kk == 0, kk == KD - 1)
                    ins.then_inc(sub_used, 1)

            def down(i0, turn, k0, banks=2):
                for i in range(4):
                    pe.wait_ge(lo_made, 12 * turn + (i0 + k0 + i + 1))
                    slot = (i0 + k0 + i) % SUB_SLOTS
                    for k in range(2):
                        kk = 2 * (i % 2) + k
                        ins = three(ps[:, banks + i // 2, :], hid_t_hi[:, kk, :], hid_t_lo[:, kk, :],
                                    w_hi[:, slot, k, :], w_lo[:, slot, k, :], kk == 0, kk == 3)
                    ins.then_inc(sub_used, 1)

            def w1_of(b, odd, halves, i0, turn, first=False):
                if not first:
                    pe.wait_ge(s("silu"), b)
                up(i0, turn, 0, ps[:, 0, :], odd, halves)

            def w3_of(b, odd, i0, turn, first=False):
                if not first:
                    pe.wait_ge(s("hid_lo"), b)
                up(i0, turn, 4, ps[:, 1, :], odd)

            def w2_of(b, n, i0, turn, k0, first=False):
                pe.wait_ge(s("hid_lo"), b + 1)
                if not first:
                    pe.wait_ge(s("y_left"), n)
                    pe.wait_ge(s("y_right"), n)
                down(i0, turn, k0)

            i0, i1 = MIX_SUBS, MIX_SUBS + 8
            gather(0, 0, 1, first=True)
            gather(1, 1, first=True)
            w1_of(0, False, 2, i0, 0, first=True)
            gather(2, 0, 2)
            w3_of(0, False, i0, 0, first=True)

            def body(e, odd, pair, first=False, more_to_come=True):
                turn_hid(e - 1, first)
                w1_of(e, odd, 2 * pair + 2, i1, e - 1)
                if more_to_come:
                    gather(e + 2, int(odd), None if odd else pair + 2)
                w3_of(e, odd, i1, e - 1)
                w2_of(e - 1, e - 1, i1, e - 1, 8, first)

            body(1, True, 0, first=True)
            with pe.Fori(1, NE // 2 - 1) as pair:
                body(2 * pair, False, pair)
                body(2 * pair + 1, True, pair)
            body(NE - 2, False, NE // 2 - 1, more_to_come=False)
            body(NE - 1, True, NE // 2 - 1, more_to_come=False)
            turn_hid(NE - 1)
            pe.wait_ge(s("hid_lo"), NE)
            down(i1, NE - 1, 0, banks=4)

            pe.wait_ge(s("extras_known"), 1)
            pe.wait_ge(s("y_last"), 2)
            n_extra = pe.value_load(xtra_i[0:1, 8:9], min_val=0, max_val=EXTRAS)
            with pe.If(n_extra > 0):
                with pe.Fori(0, EXTRAS) as j:
                    with pe.If(n_extra > j):
                        b = NE + j
                        ix = XTRA_BASE[1]
                        gather(NE + 2 * j, 0, NE // 2 + 1 + j)
                        gather(NE + 2 * j + 1, 1)
                        w1_of(b, False, NE + 2 * j + 2, ix, j)
                        w3_of(b, False, ix, j)
                        turn_hid(b)
                        w2_of(b, NE - 1 + j, ix, j, 8)


_INS = ["x", "norm1_g", "w_in", "conv_a_w", "w_a_out", "conv_b_w", "conv_b_b", "lru_wa", "lru_ba", "lru_wx",
        "lru_bx", "lru_lambda", "w_b_out", "pool_w", "pool_scale", "w_c_out", "w_o", "norm2_g", "router_grp_w",
        "router_grp_b", "router_exp_w", "router_exp_b", "moe_w1", "moe_w3", "moe_w2", "final_g"]


def kernel(**inputs):
    import numpy as _np
    import concourse.bacc as _bacc
    from concourse import mybir as _mybir
    from concourse.bass_utils import run_bass_kernel_spmd as _run

    nc = _bacc.Bacc("TRN2", target_bir_lowering=False, num_devices=1)
    arrays, args = {}, []
    for name in _INS:
        a = _np.ascontiguousarray(inputs[name])
        arrays[f"in_{name}_dram"] = a
        args.append(nc.dram_tensor(f"in_{name}_dram", a.shape, _mybir.dt.from_np(a.dtype), kind="ExternalInput").ap())
    args.append(nc.dram_tensor("out_0_dram", (1, SEQ, D), F32, kind="ExternalOutput").ap())
    trunk(nc, *args)
    r = _run(nc, [arrays], core_ids=[0])
    return r.results[0]["out_0_dram"]
```
